# Optimizing a Trainium2 kernel written in Bass

```python
import jax, jax.numpy as jnp
from jax import lax
import numpy as np

D_MODEL = 1024
BATCH = 1
SEQ = 2048
DEPTH = 1

CHUNK = 64
EXPAND = 2
D_MIX = EXPAND * D_MODEL
D_ATTN = D_MIX // 2
D_RET = D_MIX - D_ATTN
ATT_HEAD_DIM = 64
ATT_HEADS = D_ATTN // ATT_HEAD_DIM
ATT_KV_HEADS = 4
ATT_GROUP = ATT_HEADS // ATT_KV_HEADS
WINDOW = 128
WINDOW_CHUNKS = WINDOW // CHUNK
RET_HEADS = 8
RET_V_DIM = D_RET // RET_HEADS
RET_QK_DIM = RET_V_DIM // 2
EPS = 1e-6

SPLIT_SIZES = (
    D_ATTN,
    ATT_KV_HEADS * ATT_HEAD_DIM,
    ATT_KV_HEADS * ATT_HEAD_DIM,
    D_ATTN,
    RET_HEADS * RET_QK_DIM,
    RET_HEADS * RET_QK_DIM,
    D_RET,
    D_RET,
)
D_IN_PROJ = sum(SPLIT_SIZES)
SPLIT_POINTS = tuple(sum(SPLIT_SIZES[:i + 1]) for i in range(len(SPLIT_SIZES) - 1))

kernel_name = "hybrid_swa_retention_block"

def rms_norm(x, g):
    xf = x.astype(jnp.float32)
    y = xf * lax.rsqrt(jnp.mean(xf * xf, axis=-1, keepdims=True) + EPS) * g.astype(jnp.float32)
    return y.astype(x.dtype)

def window_attention(q, k, v, q_gain, k_gain, sinks):
    b, s = q.shape[0], q.shape[1]
    nc = s // CHUNK
    wc = WINDOW_CHUNKS * CHUNK
    q = rms_norm(q, q_gain)
    k = rms_norm(k, k_gain)
    qb = q.reshape(b, nc, CHUNK, ATT_KV_HEADS, ATT_GROUP, ATT_HEAD_DIM)

    def band(t):
        t = t.reshape(b, nc, CHUNK, ATT_KV_HEADS, ATT_HEAD_DIM)
        tp = jnp.pad(t, ((0, 0), (WINDOW_CHUNKS - 1, 0), (0, 0), (0, 0), (0, 0)))
        return jnp.concatenate([tp[:, i:i + nc] for i in range(WINDOW_CHUNKS)], axis=2)

    kb, vb = band(k), band(v)
    scale = ATT_HEAD_DIM ** -0.5
    scores = jnp.einsum('bnqhgd,bnkhd->bnhgqk', qb, kb).astype(jnp.float32) * scale

    slopes = 2.0 ** (-8.0 * (jnp.arange(ATT_HEADS, dtype=jnp.float32) + 1.0) / ATT_HEADS)
    qi = jnp.arange(CHUNK, dtype=jnp.float32)[:, None] + float((WINDOW_CHUNKS - 1) * CHUNK)
    ki = jnp.arange(wc, dtype=jnp.float32)[None, :]
    dist = jnp.abs(qi - ki)
    bias = -slopes.reshape(ATT_KV_HEADS, ATT_GROUP)[:, :, None, None] * dist
    key_pos = (jnp.arange(nc)[:, None] * CHUNK + jnp.arange(wc)[None, :]
               - (WINDOW_CHUNKS - 1) * CHUNK)
    valid = (key_pos >= 0)[None, :, None, None, None, :]
    scores = jnp.where(valid, scores + bias, -1e30)

    sink = sinks.astype(jnp.float32).reshape(ATT_KV_HEADS, ATT_GROUP)[None, None, :, :, None, None]
    m = jnp.maximum(jnp.max(scores, axis=-1, keepdims=True), sink)
    e = jnp.exp(scores - m)
    p = e / (jnp.sum(e, axis=-1, keepdims=True) + jnp.exp(sink - m))
    out = jnp.einsum('bnhgqk,bnkhd->bnqhgd', p.astype(vb.dtype), vb)
    return out.reshape(b, s, D_ATTN)

def retention(q, k, v, gn_gain):
    b, s = q.shape[0], q.shape[1]
    nc = s // CHUNK
    f32 = jnp.float32
    log_g = jnp.log1p(-(2.0 ** (-5.0 - jnp.arange(RET_HEADS, dtype=f32))))
    qc = q.astype(f32).reshape(b, nc, CHUNK, RET_HEADS, RET_QK_DIM)
    kc = k.astype(f32).reshape(b, nc, CHUNK, RET_HEADS, RET_QK_DIM) * (RET_QK_DIM ** -0.5)
    vc = v.astype(f32).reshape(b, nc, CHUNK, RET_HEADS, RET_V_DIM)
    idx = jnp.arange(CHUNK, dtype=f32)

    dmat = jnp.exp(log_g[:, None, None] * jnp.abs(idx[:, None] - idx[None, :]))
    a = jnp.einsum('bnihd,bnjhd->bnhij', qc, kc) * dmat
    intra = jnp.einsum('bnhij,bnjhe->bnihe', a, vc)

    wk = jnp.exp(log_g[None, :] * (CHUNK - 1.0 - idx)[:, None])
    summ = jnp.einsum('bnjhd,jh,bnjhe->nbhde', kc, wk, vc)
    g_chunk = jnp.exp(log_g * CHUNK)[None, :, None, None]

    def step(r, s_i):
        return g_chunk * r + s_i, r

    r0 = jnp.zeros((b, RET_HEADS, RET_QK_DIM, RET_V_DIM), f32)
    _, r_prev = lax.scan(step, r0, summ)
    wq = jnp.exp(log_g[None, :] * (idx + 1.0)[:, None])
    cross = jnp.einsum('bnihd,ih,nbhde->bnihe', qc, wq, r_prev)

    o = (intra + cross).reshape(b, s, RET_HEADS, RET_V_DIM)
    mu = jnp.mean(o, axis=-1, keepdims=True)
    var = jnp.mean(jnp.square(o - mu), axis=-1, keepdims=True)
    o = (o - mu) * lax.rsqrt(var + EPS)
    o = o.reshape(b, s, D_RET) * gn_gain.astype(f32)
    return o.astype(q.dtype)

def setup_inputs(seed: int = 0) -> dict:
    key = jax.random.key(seed)
    ks = jax.random.split(key, 8)
    f32 = jnp.float32
    x = jax.random.normal(ks[0], (BATCH, SEQ, D_MODEL), f32)
    norm_gain = 1.0 + 0.02 * jax.random.normal(ks[1], (D_MODEL,), f32)
    w_in = jax.random.normal(ks[2], (D_MODEL, D_IN_PROJ), f32) * D_MODEL ** -0.5
    q_norm_gain = 1.0 + 0.02 * jax.random.normal(ks[3], (ATT_HEAD_DIM,), f32)
    k_norm_gain = 1.0 + 0.02 * jax.random.normal(ks[4], (ATT_HEAD_DIM,), f32)
    sink_logits = 0.5 * jax.random.normal(ks[5], (ATT_HEADS,), f32)
    ret_norm_gain = 1.0 + 0.02 * jax.random.normal(ks[6], (D_RET,), f32)
    w_out = jax.random.normal(ks[7], (D_MIX, D_MODEL), f32) * D_MIX ** -0.5
    return {"x": x, "norm_gain": norm_gain, "w_in": w_in, "q_norm_gain": q_norm_gain,
            "k_norm_gain": k_norm_gain, "sink_logits": sink_logits,
            "ret_norm_gain": ret_norm_gain, "w_out": w_out}

def reference(x, norm_gain, w_in, q_norm_gain, k_norm_gain, sink_logits, ret_norm_gain, w_out):
    b, s, _ = x.shape
    for _layer in range(DEPTH):
        h = rms_norm(x, norm_gain)
        proj = jnp.einsum('bsd,de->bse', h, w_in)
        aq, ak, av, ag, rq, rk, rv, rg = jnp.split(proj, SPLIT_POINTS, axis=-1)
        attn = window_attention(
            aq.reshape(b, s, ATT_HEADS, ATT_HEAD_DIM),
            ak.reshape(b, s, ATT_KV_HEADS, ATT_HEAD_DIM),
            av.reshape(b, s, ATT_KV_HEADS, ATT_HEAD_DIM),
            q_norm_gain, k_norm_gain, sink_logits)
        ret = retention(
            rq.reshape(b, s, RET_HEADS, RET_QK_DIM),
            rk.reshape(b, s, RET_HEADS, RET_QK_DIM),
            rv.reshape(b, s, RET_HEADS, RET_V_DIM),
            ret_norm_gain)
        mixed = jnp.concatenate([attn * jax.nn.silu(ag), ret * jax.nn.silu(rg)], axis=-1)
        x = x + jnp.einsum('bse,ed->bsd', mixed, w_out).astype(x.dtype)
    return x


_drawn_inputs = setup_inputs


def setup_inputs(seed=0):
    import zlib

    import numpy as np

    out = dict(_drawn_inputs(seed))
    spreads = {}
    factors = {'norm_gain': 3.077,
     'q_norm_gain': 8.0,
     'k_norm_gain': 8.0,
     'sink_logits': 8.0,
     'ret_norm_gain': 7.063}
    for name, (base, spread) in spreads.items():
        noise = np.random.default_rng([zlib.crc32(name.encode()), seed]).standard_normal(out[name].shape)
        drawn = base * np.exp(spread * noise) if base else spread * noise
        out[name] = __import__('jax').numpy.asarray(drawn.astype(out[name].dtype))
    for name, factor in factors.items():
        out[name] = (out[name] * factor).astype(out[name].dtype)
    return out
```

```python
from contextlib import ExitStack

import concourse.bass as bass
from concourse import mybir

F32 = mybir.dt.float32
F32R = mybir.dt.float32r
ALU = mybir.AluOpType
ACT = mybir.ActivationFunctionType
AX = mybir.AxisListType

P = 128
SEQ, DM = 2048, 1024
CHUNK = 64
HD = 64
HEADS, KVH = 16, 4
RET_HEADS, RV = 8, 128
EPS = 1e-6
BLK = 512
NB = SEQ // BLK
NT = BLK // P
KT = DM // P
NU = KVH
C_AQ, C_AK, C_AV, C_AG, C_RQ, C_RK, C_RV, C_RG = 0, 1024, 1280, 1536, 2560, 3072, 3584, 4608
D_ATTN = 1024

J_QKV, J_AG, J_RQ, J_RK, J_RVG, J_OUT, JOBS = 0, 4, 6, 7, 8, 12, 20
W_SUBS = 8
W_PANELS = 4
W_WIDTH = [384, 512, 512, 512]
W_DMAS = [3, 3, 2, 1]
STEPS = {
    3: [("TQ", 0)], 4: [("TQ", 1)], 5: [("TQ", 2), ("S", 0)], 6: [("TQ", 3), ("S", 1)],
    7: [("PT", 0), ("S", 2)], 8: [("PT", 1), ("PV", 0), ("S", 3)],
    9: [("PT", 2), ("PV", 1), ("KT", 0), ("A", 0)],
    10: [("PT", 3), ("PV", 2), ("I", 0), ("KT", 1), ("A", 1)],
    11: [("PV", 3), ("I", 1), ("KT", 2), ("A", 2), ("MT", 0)],
    12: [("I", 2), ("KT", 3), ("A", 3), ("MT", 1)],
    14: [("I", 3), ("MT", 2)], 16: [("MT", 3)],
}
CREDIT_JOB, CREDIT_ACC, CREDIT_SAVE, CREDIT_UPD, CREDIT_WL = JOBS, 2 * NT, 1, NT, 32


def nth(n, per_unit, j):
    return n * per_unit + (j + 1)


def build(nc, x, norm_gain, w_in, q_gain, k_gain, sinks, ret_gain, w_out, c_bias0, c_bias, c_ret, c_ident, out):
    w_in_v = w_in.rearrange("(k p) n -> p k n", p=P)
    w_out_v = w_out.rearrange("(k p) n -> p k n", p=P)
    sinks_v = sinks.rearrange("(h a) -> a h", a=2)

    with ExitStack() as ctx:
        def sb(name, shape, dt=F32):
            return ctx.enter_context(nc.sbuf_tensor(name, shape, dt))

        def pb(name):
            return ctx.enter_context(nc.psum_tensor(name, [P, 512], F32))

        def sem(name):
            return ctx.enter_context(nc.semaphore(name))

        hTH, hTL = sb("hTH", [P, KT, BLK], F32R), sb("hTL", [P, KT, BLK], F32R)
        wH = [sb(f"wH{i}", [P, W_SUBS, 512], F32R) for i in range(2)]
        wL = [sb(f"wL{i}", [P, W_SUBS, 512], F32R) for i in range(2)]
        stage = sb("stage", [P, 2, 2, 512])
        acc = sb("acc", [P, NT, DM])
        mxH, mxL = sb("mxH", [P, 4, BLK], F32R), sb("mxL", [P, 4, BLK], F32R)
        gate = sb("gate", [P, 2 * BLK])
        sx = sb("sx", [P, 2 * BLK])
        xbuf = [gate, sx]
        th = sb("th", [P, BLK])
        raw = sb("raw", [P, 2, 384])
        qn = sb("qn", [P, 2, 384])
        qS = sb("qS", [P, NT, 4, P], F32R)
        kHH, kLL = sb("kHH", [P, CHUNK + BLK], F32R), sb("kLL", [P, CHUNK + BLK], F32R)
        voH, voL = sb("voH", [P, NT, HD], F32R), sb("voL", [P, NT, HD], F32R)
        veH, veL = sb("veH", [P, NT, HD], F32R), sb("veL", [P, NT, HD], F32R)
        kcar = sb("kcar", [P, NU, 2, CHUNK], F32R)
        vcar = sb("vcar", [P, NU, 2, HD], F32R)
        pTH, pTL = sb("pTH", [P, 512], F32R), sb("pTL", [P, 512], F32R)
        mixr = sb("mixr", [P, 2, P])
        bias = sb("bias", [P, 768])
        sink, nsink = sb("sink", [P, 2]), sb("nsink", [P, 2])
        m4, nm4, d4, den, es, rc = (sb(n_, [P, 4]) for n_ in ("m4", "nm4", "d4", "den", "es", "rc"))
        ss, ms, rstd = sb("ss", [P, 5]), sb("ms", [P, 5]), sb("rstd", [P, 5])
        mhalf = sb("mhalf", [P, 8])
        rqH, rqL = sb("rqH", [P, 2, BLK], F32R), sb("rqL", [P, 2, BLK], F32R)
        rkH, rkL = sb("rkH", [P, BLK], F32R), sb("rkL", [P, BLK], F32R)
        kr = sb("kr", [P, BLK])
        rvH, rvL = sb("rvH", [P, 2, 2 * RV], F32R), sb("rvL", [P, 2, 2 * RV], F32R)
        gg = sb("gg", [P, 2, 2 * RV])
        kwr, kwH, kwL = sb("kwr", [P, P]), sb("kwH", [P, P], F32R), sb("kwL", [P, P], F32R)
        amr, aH, aL = sb("amr", [P, 2 * P]), sb("aH", [P, 2 * P], F32R), sb("aL", [P, 2 * P], F32R)
        rst = sb("rst", [P, NU, RV])
        rcur, rH, rL = sb("rcur", [P, RV]), sb("rH", [P, RV], F32R), sb("rL", [P, RV], F32R)
        oraw, mr = sb("oraw", [P, 2, RV]), sb("mr", [P, 2, RV])
        st, mv, ve, grs = sb("st", [P, 2, 6]), sb("mv", [P, 2, 2]), sb("ve", [P, 2]), sb("grs", [P, 2])
        cret = sb("cret", [P, 513])
        cD, cwq, cwk, cg = cret[:, 0:256], cret[:, 256:384], cret[:, 384:512], cret[:, 512:513]
        gain = sb("gain", [P, 2 * RV])
        ident = sb("ident", [P, P])
        ngain = sb("ngain", [P, KT])
        qkg = sb("qkg", [P, 2])
        xss, xms, xr = sb("xss", [P, 2]), sb("xms", [P, 2]), sb("xr", [P, 1])

        jb = [pb("jb0"), pb("jb1")]
        tr, sbk, ptb, ob, ab, ro = pb("tr"), pb("sbk"), pb("ptb"), pb("ob"), pb("ab"), pb("ro")

        names = """s_ident s_mhalf s_zero s_x0 s_x1 s_xsq s_xss s_xms s_xr s_xn s_xT s_xH s_xL s_accin s_store
            s_w0 s_w1 s_wh s_wl s_job s_cattn s_cret s_raw s_sq s_voh s_ms s_rstd s_qn s_tq s_tqh s_tql
            s_s s_x s_nm s_exp s_pn s_pt s_pth s_ptl s_pv s_mixr s_mixh s_mixl s_agt s_gate
            s_qpr s_rqh s_rql s_rkh s_rkl s_rvt s_rvg s_kt s_kw s_kwh s_kwl s_a s_am s_ah s_al
            s_i s_rupd s_oc s_rh s_rl s_rcur s_var s_grs s_mr s_mt s_mth s_mtl s_acc s_nsink s_carin s_carry
            s_dve s_dvex""".split()
        S = {name: sem(name) for name in names}
        s_x = [S["s_x0"], S["s_x1"]]
        s_w = [S["s_w0"], S["s_w1"]]
        block = ctx.enter_context(nc.Block())

        @block.sync
        def _(sp):
            for dst, src in ((ident[:, :], c_ident), (ngain[:, :], norm_gain.rearrange("(k p) -> p k", p=P))):
                sp.dma_start(dst, src, allow_slow_non_contiguous=True).then_inc(S["s_ident"], 16)
            for half in range(2):
                rows = slice(half * HD, half * HD + HD)
                sp.dma_start(qkg[rows, 0:1], q_gain.rearrange("(d o) -> d o", o=1)).then_inc(S["s_ident"], 16)
                sp.dma_start(qkg[rows, 1:2], k_gain.rearrange("(d o) -> d o", o=1)).then_inc(S["s_ident"], 16)

            def stage_dma(n, u, p, c):
                i = 4 * p + c
                sp.wait_ge(S["s_wl"], nth(n, 32, 2 * (i - 2) + 1) + CREDIT_WL)
                q = s_w[c % 2]
                dst = stage[:, c % 2]
                if p == 0:
                    for at, w, col in ((0, 256, C_AQ), (256, 64, C_AK), (320, 64, C_AV)):
                        sp.dma_start(dst[:, :, at:at + w],
                                     w_in_v[:, 2 * c:2 * c + 2, bass.ds(u * w + col, w)]).then_inc(q, 16)
                elif p == 1:
                    for at, w, col in ((0, 256, C_AG), (256, 128, C_RQ), (384, 128, C_RK)):
                        sp.dma_start(dst[:, :, at:at + w],
                                     w_in_v[:, 2 * c:2 * c + 2, bass.ds(u * w + col, w)]).then_inc(q, 16)
                elif p == 2:
                    for at, w, col in ((0, 256, C_RV), (256, 256, C_RG)):
                        sp.dma_start(dst[:, :, at:at + w],
                                     w_in_v[:, 2 * c:2 * c + 2, bass.ds(u * w + col, w)]).then_inc(q, 16)
                else:
                    base = (c % 2) * KT
                    sp.dma_start(dst[:, :, :],
                                 w_out_v[:, bass.ds(u * 2 + base, 2), (c // 2) * 512:(c // 2 + 1) * 512]).then_inc(q, 16)

            with sp.Fori(0, NB) as b:
                sp.wait_ge(S["s_carry"], 4 * b + 1)
                for t in range(NT):
                    if t >= 2:
                        sp.wait_ge(S["s_xT"], nth(b, 8, 2 * (t - 2) + 1))
                    sp.dma_start(xbuf[t % 2][:, :], x[0, bass.ds(b * BLK + t * P, P), :]).then_inc(s_x[t % 2], 16)
                sp.wait_ge(S["s_store"], 16 * b + 16)
                sp.dma_start(acc[:, :, :], x[0, bass.ds(b * BLK, BLK), :].rearrange("(t p) d -> p t d", p=P)
                             ).then_inc(S["s_accin"], 16)
                with sp.Fori(0, NU) as u:
                    n = b * NU + u
                    for c in range(4):
                        stage_dma(n, u, 0, c)
                    sp.wait_ge(S["s_carry"], n + 1)
                    sp.dma_start(bias[:, 0:256], c_bias0[b, u]).then_inc(S["s_cattn"], 16)
                    sp.dma_start(bias[:, 256:768], c_bias[u]).then_inc(S["s_cattn"], 16)
                    for a in range(2):
                        sp.dma_start(sink[a * 64:a * 64 + 64, :],
                                     sinks_v[a, bass.ds(u * 2, 2)].partition_broadcast(64),
                                     allow_slow_non_contiguous=True).then_inc(S["s_cattn"], 16)
                    sp.wait_ge(S["s_rupd"], 4 * n + CREDIT_UPD)
                    sp.dma_start(cret[:, :], c_ret[u]).then_inc(S["s_cret"], 16)
                    sp.dma_start(gain[:, :], ret_gain[bass.ds(u * 256, 256)].partition_broadcast(P)).then_inc(S["s_cret"], 16)
                    for p in range(1, 4):
                        for c in range(4):
                            stage_dma(n, u, p, c)

        @block.gpsimd
        def _(pool):
            pool.memset(mhalf[:, :], -0.5).then_inc(S["s_mhalf"], 1)
            pool.sem_inc(S["s_wl"], CREDIT_WL)
            pool.wait_ge(S["s_mhalf"], 1)

            def wl(n, p, subs):
                for s in subs:
                    pool.wait_ge(S["s_wh"], nth(n, 32, 8 * p + s))
                    w = W_WIDTH[p]
                    pool.tensor_tensor(wL[p % 2][:, s, 0:w], stage[:, (s // 2) % 2, s % 2, 0:w],
                                       wH[p % 2][:, s, 0:w].bitcast(F32), ALU.subtract).then_inc(S["s_wl"], 1)

            def rpow(n, t):
                pool.wait_ge(S["s_ms"], nth(n, 4, t))
                pool.tensor_tensor(rstd[:, :], ms[:, :], mhalf[:, 0:5], ALU.pow).then_inc(S["s_rstd"], 1)

            def gpow(n, t):
                pool.wait_ge(S["s_var"], nth(n, 4, t))
                pool.tensor_tensor(grs[:, :], ve[:, :], mhalf[:, 0:2], ALU.pow).then_inc(S["s_grs"], 1)

            with pool.Fori(0, NB) as b:
                for t in range(NT):
                    pool.wait_ge(S["s_xms"], nth(b, 4, t))
                    pool.tensor_tensor(xr[:, :], xms[:, 1:2], mhalf[:, 0:1], ALU.pow).then_inc(S["s_xr"], 1)
                with pool.Fori(0, NU) as u:
                    n = b * NU + u
                    wl(n, 0, range(8))
                    rpow(n, 0); wl(n, 1, (0, 1, 2))
                    rpow(n, 1); wl(n, 1, (3, 4, 5))
                    rpow(n, 2); wl(n, 1, (6, 7))
                    rpow(n, 3); wl(n, 2, range(8))
                    wl(n, 3, range(0, 6))
                    gpow(n, 0); wl(n, 3, (6, 7))
                    gpow(n, 1); gpow(n, 2); gpow(n, 3)

        @block.scalar
        def _(act):
            act.wait_ge(S["s_ident"], 96)

            def wh(n, p, subs):
                for s in subs:
                    c = s // 2
                    if s == subs[0]:
                        last = {0: J_OUT - 1 - JOBS, 1: JOBS - 1 - JOBS, 2: J_AG - 1, 3: J_RK}[p]
                        act.wait_ge(S["s_job"], nth(n, JOBS, last) + CREDIT_JOB)
                    if s % 2 == 0 or s == subs[0]:
                        done = sum(2 * W_DMAS[q] for q in range(p)) + (c // 2 + 1) * W_DMAS[p]
                        act.wait_ge(s_w[c % 2], n * (16 * 18) + 16 * done)
                    w = W_WIDTH[p]
                    act.activation(wH[p % 2][:, s, 0:w], stage[:, c % 2, s % 2, 0:w], ACT.Copy).then_inc(S["s_wh"], 1)

            def qkv(n, t):
                act.wait_ge(S["s_job"], nth(n, JOBS, J_QKV + t) + CREDIT_JOB)
                if t >= 2:
                    act.wait_ge(S["s_qn"], nth(n, 4, t - 2))
                act.activation(raw[:, t % 2], jb[t % 2][:, 0:384], ACT.Copy).then_inc(S["s_raw"], 1)
                act.wait_ge(S["s_raw"], nth(n, 4, t))
                if t >= 1:
                    act.wait_ge(S["s_ms"], nth(n, 4, t - 1))
                act.activation(th[:, 0:320], raw[:, t % 2, 0:320], ACT.Square).then_inc(S["s_sq"], 1)
                act.activation(voH[:, t], raw[:, t % 2, 320:384], ACT.Copy).then_inc(S["s_voh"], 1)

            def tqh(n, t):
                act.wait_ge(S["s_tq"], nth(n, 4, t))
                for a in range(2):
                    rows = slice(a * 64, a * 64 + 64)
                    act.activation(qS[rows, t, :, a * 64:a * 64 + 64],
                                   tr[rows, 0:256].rearrange("p (c q) -> p c q", q=64), ACT.Copy, scale=qkg[rows, 0:1])
                act.activation(kHH[:, CHUNK + t * P:CHUNK + (t + 1) * P], tr[:, 256:384], ACT.Copy,
                               scale=qkg[:, 1:2]).then_inc(S["s_tqh"], 1)

            def ag(n, i):
                act.wait_ge(S["s_job"], nth(n, JOBS, J_AG + i) + CREDIT_JOB)
                if i == 0:
                    act.wait_ge(S["s_ms"], nth(n, 4, 3))
                else:
                    act.wait_ge(S["s_gate"], nth(n, 2, 0))
                act.activation(th[:, :], jb[i % 2][:, :], ACT.Tanh, scale=0.5).then_inc(S["s_agt"], 1)

            def exps(n, t):
                act.wait_ge(S["s_nm"], nth(n, 4, t))
                for i in range(4):
                    v = sx[:, (t % 2) * 512 + i * P:(t % 2) * 512 + (i + 1) * P]
                    act.activation(v, v, ACT.Exp, bias=nm4[:, i:i + 1], accum_out=den[:, i:i + 1])
                act.activation(es[:, :], d4[:, :], ACT.Exp).then_inc(S["s_exp"], 1)

            def pth(n, t):
                act.wait_ge(S["s_pt"], nth(n, 4, t))
                if t >= 1:
                    act.wait_ge(S["s_pv"], nth(n, 4, t - 1))
                act.activation(pTH[:, :], ptb[:, :], ACT.Copy).then_inc(S["s_pth"], 1)

            def rqh(n):
                act.wait_ge(S["s_qpr"], nth(n, 1, 0))
                for a in range(2):
                    rows = slice(a * 64, a * 64 + 64)
                    i = act.activation(rqH[rows, a], th[rows, :], ACT.Copy)
                i.then_inc(S["s_rqh"], 1)

            def rk(n):
                act.wait_ge(S["s_job"], nth(n, JOBS, J_RK) + CREDIT_JOB)
                act.activation(kr[:, :], jb[1][:, :], ACT.Copy)
                act.activation(rkH[:, :], jb[1][:, :], ACT.Copy).then_inc(S["s_rkh"], 1)

            def rvg(n, t):
                act.wait_ge(S["s_job"], nth(n, JOBS, J_RVG + t) + CREDIT_JOB)
                if t >= 2:
                    act.wait_ge(S["s_i"], nth(n, 4, t - 2))
                act.activation(rvH[:, t % 2], jb[t % 2][:, 0:256], ACT.Copy)
                if t == 0:
                    act.wait_ge(S["s_rql"], nth(n, 1, 0))
                else:
                    act.wait_ge(S["s_rvg"], nth(n, 4, t - 1))
                act.activation(th[:, 0:256], jb[t % 2][:, 256:512], ACT.Tanh, scale=0.5).then_inc(S["s_rvt"], 1)

            def mixh(n, t):
                act.wait_ge(S["s_mixr"], nth(n, 4, t))
                act.activation(mxH[:, 0:2, t * P:(t + 1) * P], mixr[:, :, :], ACT.Copy).then_inc(S["s_mixh"], 1)

            def kwh_ah(n, t):
                act.wait_ge(S["s_kw"], nth(n, 4, t))
                if t >= 1:
                    act.wait_ge(S["s_i"], nth(n, 4, t - 1))
                act.activation(kwH[:, :], kwr[:, :], ACT.Copy).then_inc(S["s_kwh"], 1)
                act.wait_ge(S["s_am"], nth(n, 4, t))
                act.activation(aH[:, :], amr[:, :], ACT.Copy).then_inc(S["s_ah"], 1)

            def rh(n, t):
                if t == 0:
                    act.wait_ge(S["s_rcur"], nth(n, 1, 0))
                else:
                    act.wait_ge(S["s_rupd"], nth(n, 4, t - 1) + CREDIT_UPD)
                act.activation(rH[:, :], rcur[:, :], ACT.Copy).then_inc(S["s_rh"], 1)

            def ocopy(n, t):
                act.wait_ge(S["s_rupd"], nth(n, 4, t) + CREDIT_UPD)
                if t >= 1:
                    act.wait_ge(S["s_mr"], nth(n, 4, t - 1))
                act.activation(oraw[:, :, :], ro[:, 0:256].rearrange("p (h e) -> p h e", h=2), ACT.Copy
                               ).then_inc(S["s_oc"], 1)

            def mth(n, t):
                act.wait_ge(S["s_mt"], nth(n, 4, t))
                act.activation(mxH[:, 2:4, t * P:(t + 1) * P], tr[:, 0:256].rearrange("p (h q) -> p h q", h=2),
                               ACT.Copy).then_inc(S["s_mth"], 1)

            with act.Fori(0, NB) as b:
                for t in range(NT):
                    act.wait_ge(s_x[t % 2], b * 32 + 16 * (t // 2 + 1))
                    if t >= 1:
                        act.wait_ge(S["s_xms"], nth(b, 4, t - 1))
                    for h in range(2):
                        i = act.activation((th, kr)[h][:, :], xbuf[t % 2][:, h * 512:(h + 1) * 512], ACT.Square,
                                           accum_out=xss[:, h:h + 1])
                    i.then_inc(S["s_xsq"], 1)
                    for h in range(2):
                        act.wait_ge(S["s_xT"], nth(b, 8, 2 * t + h))
                        bank = (sbk, ptb)[h]
                        for k in range(4):
                            i = act.activation(hTH[:, 4 * h + k, t * P:(t + 1) * P], bank[:, k * P:(k + 1) * P],
                                               ACT.Copy, scale=ngain[:, 4 * h + k:4 * h + k + 1])
                        i.then_inc(S["s_xH"], 1)
                with act.Fori(0, NU) as u:
                    n = b * NU + u
                    wh(n, 0, list(range(8)))
                    qkv(n, 0); wh(n, 1, [0, 1, 2])
                    qkv(n, 1); wh(n, 1, [3, 4, 5])
                    qkv(n, 2); tqh(n, 0); wh(n, 1, [6, 7])
                    qkv(n, 3); tqh(n, 1); wh(n, 2, [0, 1])
                    tqh(n, 2); ag(n, 0); wh(n, 2, [2, 3]); exps(n, 0)
                    tqh(n, 3); ag(n, 1); wh(n, 2, [4, 5]); exps(n, 1)
                    pth(n, 0); rqh(n); wh(n, 2, [6, 7]); exps(n, 2)
                    pth(n, 1); rk(n); mixh(n, 0); wh(n, 3, [0, 1]); exps(n, 3); rh(n, 0)
                    pth(n, 2); rvg(n, 0); mixh(n, 1); kwh_ah(n, 0); wh(n, 3, [2, 3])
                    pth(n, 3); rvg(n, 1); mixh(n, 2); ocopy(n, 0); rh(n, 1); kwh_ah(n, 1); wh(n, 3, [4, 5])
                    rvg(n, 2); mixh(n, 3); ocopy(n, 1); rh(n, 2); kwh_ah(n, 2); wh(n, 3, [6, 7]); mth(n, 0)
                    rvg(n, 3); ocopy(n, 2); rh(n, 3); kwh_ah(n, 3); mth(n, 1)
                    ocopy(n, 3); mth(n, 2)
                    mth(n, 3)
                act.wait_ge(S["s_acc"], b * 32 + (32 + CREDIT_ACC))
                act.dma_start(out[0, bass.ds(b * BLK, BLK), :].rearrange("(t p) d -> p t d", p=P), acc[:, :, :]
                              ).then_inc(S["s_store"], 16)
            act.wait_ge(S["s_store"], 16 * (NB + 1))

        @block.vector
        def _(v):
            UNIT_LINKS, X_LINKS = 36, NT
            link_at = {"s_dve": [0, 0], "s_dvex": [0, 0]}

            def link(ins, name="s_dve"):
                ins.then_inc(S[name], 1)
                link_at[name][0] += 1
                v.wait_ge(S[name], link_at[name][1] + link_at[name][0])

            def sub(out, a, h):
                return v.tensor_tensor(out, a, h.bitcast(F32), ALU.subtract)

            v.memset(rst[:, :, :], 0.0).then_inc(S["s_zero"], 1)
            v.memset(rqH[:, :, :].bitcast(F32), 0.0).then_inc(S["s_zero"], 1)
            v.memset(rqL[:, :, :].bitcast(F32), 0.0).then_inc(S["s_zero"], 1)
            v.memset(kcar[:, :, :, :].bitcast(F32), 0.0).then_inc(S["s_zero"], 1)
            v.memset(vcar[:, :, :, :].bitcast(F32), 0.0).then_inc(S["s_zero"], 1)
            v.sem_inc(S["s_acc"], CREDIT_ACC)
            v.sem_inc(S["s_carry"], CREDIT_SAVE)
            v.sem_inc(S["s_rupd"], CREDIT_UPD)
            v.sem_inc(S["s_store"], 16)
            v.wait_ge(S["s_zero"], 5)
            v.wait_ge(S["s_ident"], 96)

            def carry_in(n, u):
                v.wait_ge(S["s_carry"], n + 1)
                v.wait_ge(S["s_rupd"], 4 * n + CREDIT_UPD)
                v.wait_ge(S["s_cattn"], 64 * n + 64)
                v.tensor_scalar(nsink[:, :], sink[:, :], -1.0, None, ALU.mult).then_inc(S["s_nsink"], 1)
                v.tensor_copy(kHH[:, 0:CHUNK], kcar[:, bass.ds(u, 1), 0].rearrange("p o c -> p (o c)").bitcast(F32))
                v.tensor_copy(kLL[:, 0:CHUNK], kcar[:, bass.ds(u, 1), 1].rearrange("p o c -> p (o c)").bitcast(F32))
                v.tensor_copy(veH[64:128, 0], vcar[64:128, bass.ds(u, 1), 0].rearrange("p o c -> p (o c)").bitcast(F32))
                v.tensor_copy(veL[64:128, 0], vcar[64:128, bass.ds(u, 1), 1].rearrange("p o c -> p (o c)").bitcast(F32)
                              ).then_inc(S["s_carin"], 1)
                v.tensor_copy(rcur[:, :], rst[:, bass.ds(u, 1)].rearrange("p o c -> p (o c)")).then_inc(S["s_rcur"], 1)

            def qkv(n, u, t):
                v.wait_ge(S["s_sq"], nth(n, 4, t))
                link(v.tensor_reduce(ss[:, :], th[:, 0:320].rearrange("p (h d) -> p h d", d=HD), AX.X, ALU.add))
                v.tensor_scalar(ms[:, :], ss[:, :], 1.0 / HD, EPS, ALU.mult, ALU.add).then_inc(S["s_ms"], 1)
                v.wait_ge(S["s_voh"], nth(n, 4, t))
                link(sub(voL[:, t], raw[:, t % 2, 320:384], voH[:, t]))
                for vo, vx, part in ((voH, veH, 0), (voL, veL, 1)):
                    v.tensor_copy(vx[0:64, t], vo[0:64, t].bitcast(F32))
                    if t < NT - 1:
                        v.tensor_copy(vx[64:128, t + 1], vo[64:128, t].bitcast(F32))
                    else:
                        v.tensor_copy(vcar[64:128, bass.ds(u, 1), part].rearrange("p o c -> p (o c)"),
                                      vo[64:128, t].bitcast(F32))
                if t >= 2:
                    v.wait_ge(S["s_tq"], nth(n, 4, t - 2))
                v.wait_ge(S["s_rstd"], nth(n, 4, t))
                v.tensor_tensor(qn[:, t % 2, 0:320].rearrange("p (h d) -> p h d", d=HD),
                                raw[:, t % 2, 0:320].rearrange("p (h d) -> p h d", d=HD),
                                rstd[:, :].unsqueeze(2).broadcast_to([P, 5, HD]), ALU.mult)
                v.tensor_tensor(qn[:, t % 2, 320:384], raw[:, t % 2, 256:320],
                                rstd[:, 4:5].broadcast_to([P, HD]), ALU.mult).then_inc(S["s_qn"], 1)

            def tql(n, t):
                v.wait_ge(S["s_tqh"], nth(n, 4, t))
                for a in range(2):
                    rows, other = slice(a * 64, a * 64 + 64), slice(64 - a * 64, 128 - a * 64)
                    v.scalar_tensor_tensor(out=qS[other, t, :, a * 64:a * 64 + 64],
                                           in0=tr[rows, 0:256].rearrange("p (c q) -> p c q", q=64),
                                           scalar=qkg[rows, 0:1], in1=qS[rows, t, :, a * 64:a * 64 + 64].bitcast(F32),
                                           op0=ALU.mult, op1=ALU.subtract)
                cols = slice(CHUNK + t * P, CHUNK + (t + 1) * P)
                v.scalar_tensor_tensor(out=kLL[:, cols], in0=tr[:, 256:384], scalar=qkg[:, 1:2],
                                       in1=kHH[:, cols].bitcast(F32), op0=ALU.mult, op1=ALU.subtract
                                       ).then_inc(S["s_tql"], 1)

            def part1(n, t):
                v.wait_ge(S["s_s"], nth(n, 4, t))
                if t == 0:
                    v.wait_ge(S["s_nsink"], nth(n, 1, 0))
                if t >= 2:
                    v.wait_ge(S["s_pt"], nth(n, 4, t - 2))
                xs = sx[:, (t % 2) * 512:(t % 2 + 1) * 512]
                bt = bias[:, 0:512] if t == 0 else bias[:, 256:768]
                v.scalar_tensor_tensor(out=xs, in0=sbk[:, :], scalar=HD ** -0.5, in1=bt, op0=ALU.mult, op1=ALU.add
                                       ).then_inc(S["s_x"], 1)
                v.wait_ge(S["s_x"], nth(n, 4, t))
                link(v.tensor_reduce(m4[:, :], xs.rearrange("p (r k) -> p r k", k=P), AX.X, ALU.max))
                b2 = lambda a: a[:, :].unsqueeze(1).broadcast_to([P, 2, 2])
                q4 = lambda a: a[:, :].rearrange("p (c h) -> p c h", c=2)
                link(v.scalar_tensor_tensor(out=q4(nm4), in0=q4(m4), scalar=-1.0, in1=b2(nsink), op0=ALU.mult,
                                            op1=ALU.min))
                v.tensor_tensor(q4(d4), q4(nm4), b2(sink), ALU.add).then_inc(S["s_nm"], 1)

            def part2(n, t):
                v.wait_ge(S["s_exp"], nth(n, 4, t))
                link(v.tensor_tensor(den[:, :], den[:, :], es[:, :], ALU.add))
                link(v.reciprocal(rc[:, :], den[:, :]))
                xs = sx[:, (t % 2) * 512:(t % 2 + 1) * 512].rearrange("p (r k) -> p r k", k=P)
                v.scalar_tensor_tensor(out=xs, in0=xs, scalar=0.5, in1=rc[:, :].unsqueeze(2).broadcast_to([P, 4, P]),
                                       op0=ALU.mult, op1=ALU.mult).then_inc(S["s_pn"], 1)

            def agg(n, i):
                v.wait_ge(S["s_agt"], nth(n, 2, i))
                v.scalar_tensor_tensor(out=gate[:, i * 512:(i + 1) * 512], in0=th[:, :], scalar=1.0, in1=jb[i % 2][:, :],
                                       op0=ALU.add, op1=ALU.mult).then_inc(S["s_gate"], 1)

            def ptl(n, t):
                v.wait_ge(S["s_pth"], nth(n, 4, t))
                sub(pTL[:, :], ptb[:, :], pTH[:, :]).then_inc(S["s_ptl"], 1)

            def mix(n, t):
                v.wait_ge(S["s_pv"], nth(n, 4, t))
                if t == 0:
                    v.wait_ge(S["s_gate"], nth(n, 2, 1))
                else:
                    v.wait_ge(S["s_mixl"], nth(n, 4, t - 1))
                for a in range(2):
                    rows = slice(a * 64, a * 64 + 64)
                    i = v.tensor_tensor(mixr[rows, :, :],
                                        ob[0:64, :].rearrange("p (h a q) -> p h a q", h=2, a=2)[:, :, a],
                                        gate[rows, :].rearrange("p (h s) -> p h s", h=2)[:, :, t * P:(t + 1) * P],
                                        ALU.mult)
                i.then_inc(S["s_mixr"], 1)

            def mixl(n, t):
                v.wait_ge(S["s_mixh"], nth(n, 4, t))
                sub(mxL[:, 0:2, t * P:(t + 1) * P], mixr[:, :, :], mxH[:, 0:2, t * P:(t + 1) * P]
                    ).then_inc(S["s_mixl"], 1)

            def rq_decay(n):
                v.wait_ge(S["s_job"], nth(n, JOBS, J_RQ) + CREDIT_JOB)
                v.wait_ge(S["s_cret"], 32 * n + 32)
                v.tensor_tensor(th[:, :].rearrange("p (t i) -> p t i", i=P),
                                jb[0][:, :].rearrange("p (t i) -> p t i", i=P),
                                cwq.unsqueeze(1).broadcast_to([P, NT, P]), ALU.mult).then_inc(S["s_qpr"], 1)

            def rql(n):
                v.wait_ge(S["s_rqh"], nth(n, 1, 0))
                for a in range(2):
                    rows = slice(a * 64, a * 64 + 64)
                    i = sub(rqL[rows, a], th[rows, :], rqH[rows, a])
                i.then_inc(S["s_rql"], 1)

            def rkl(n):
                v.wait_ge(S["s_rkh"], nth(n, 1, 0))
                sub(rkL[:, :], jb[1][:, :], rkH[:, :]).then_inc(S["s_rkl"], 1)

            def rvg(n, t):
                v.wait_ge(S["s_rvt"], nth(n, 4, t))
                bank, g = jb[t % 2], gg[:, t % 2]
                sub(rvL[:, t % 2], bank[:, 0:256], rvH[:, t % 2])
                if t >= 2:
                    v.wait_ge(S["s_mr"], nth(n, 4, t - 2))
                v.scalar_tensor_tensor(out=g, in0=th[:, 0:256], scalar=1.0, in1=bank[:, 256:512], op0=ALU.add,
                                       op1=ALU.mult).then_inc(S["s_rvg"], 1)

            def kw_am(n, t):
                v.wait_ge(S["s_kt"], nth(n, 4, t))
                if t >= 1:
                    v.wait_ge(S["s_kwl"], nth(n, 4, t - 1))
                    v.wait_ge(S["s_al"], nth(n, 4, t - 1))
                v.tensor_tensor(kwr[:, :], tr[:, 0:128], cwk, ALU.mult).then_inc(S["s_kw"], 1)
                v.wait_ge(S["s_a"], nth(n, 4, t))
                v.tensor_tensor(amr[:, :], ab[:, 0:256], cD, ALU.mult).then_inc(S["s_am"], 1)

            def kwl_al(n, t):
                v.wait_ge(S["s_kwh"], nth(n, 4, t))
                sub(kwL[:, :], kwr[:, :], kwH[:, :]).then_inc(S["s_kwl"], 1)
                v.wait_ge(S["s_ah"], nth(n, 4, t))
                sub(aL[:, :], amr[:, :], aH[:, :]).then_inc(S["s_al"], 1)

            def rl(n, t):
                v.wait_ge(S["s_rh"], nth(n, 4, t))
                sub(rL[:, :], rcur[:, :], rH[:, :]).then_inc(S["s_rl"], 1)

            def rupd(n, t, u=None):
                v.wait_ge(S["s_i"], nth(n, 4, t))
                for a in range(2):
                    rows = slice(a * 64, a * 64 + 64)
                    new = rcur[rows, :] if t < NT - 1 else rst[rows, bass.ds(u, 1)].rearrange("p o c -> p (o c)")
                    i = v.scalar_tensor_tensor(out=new, in0=rcur[rows, :], scalar=cg[rows, :],
                                               in1=ro[rows, 256 + a * P:256 + (a + 1) * P], op0=ALU.mult, op1=ALU.add)
                i.then_inc(S["s_rupd"], 1)

            def gn(n, t):
                v.wait_ge(S["s_oc"], nth(n, 4, t))
                for h in range(2):
                    i = v.bn_stats(st[:, h], oraw[:, h])
                link(i)
                v.scalar_tensor_tensor(out=gg[:, t % 2], in0=gg[:, t % 2], scalar=0.5, in1=gain[:, :], op0=ALU.mult,
                                       op1=ALU.mult)
                for h in range(2):
                    i = v.bn_aggr(mv[:, h], st[:, h])
                link(i)
                v.tensor_scalar(ve[:, :], mv[:, :, 1], EPS, None, ALU.add).then_inc(S["s_var"], 1)
                v.wait_ge(S["s_grs"], nth(n, 4, t))
                for h in range(2):
                    i = v.tensor_scalar(oraw[:, h], oraw[:, h], mv[:, h, 0:1], grs[:, h:h + 1], ALU.subtract, ALU.mult)
                link(i)
                if t >= 1:
                    v.wait_ge(S["s_mt"], nth(n, 4, t - 1))
                v.tensor_tensor(mr[:, :, :], oraw[:, :, :], gg[:, t % 2].rearrange("p (h e) -> p h e", h=2), ALU.mult
                                ).then_inc(S["s_mr"], 1)

            def mtl(n, t):
                v.wait_ge(S["s_mth"], nth(n, 4, t))
                sub(mxL[:, 2:4, t * P:(t + 1) * P], tr[:, 0:256].rearrange("p (h q) -> p h q", h=2),
                    mxH[:, 2:4, t * P:(t + 1) * P]).then_inc(S["s_mtl"], 1)

            def add(n, b, i):
                v.wait_ge(S["s_job"], nth(n, JOBS, J_OUT + i) + CREDIT_JOB)
                if i == 0:
                    v.wait_ge(S["s_accin"], 16 * b + 16)
                v.wait_ge(S["s_acc"], n * 8 + (i + 1))
                a = acc[:, i // 2, (i % 2) * 512:(i % 2 + 1) * 512]
                v.tensor_tensor(a, a, jb[i % 2][:, :], ALU.add).then_inc(S["s_acc"], 1)

            with v.Fori(0, NB) as b:
                link_at["s_dvex"] = [0, b * X_LINKS]
                for t in range(NT):
                    v.wait_ge(S["s_xsq"], nth(b, 4, t))
                    link(v.tensor_tensor(xms[:, 0:1], xss[:, 0:1], xss[:, 1:2], ALU.add), "s_dvex")
                    v.tensor_scalar(xms[:, 1:2], xms[:, 0:1], 1.0 / DM, EPS, ALU.mult, ALU.add).then_inc(S["s_xms"], 1)
                    v.wait_ge(S["s_xr"], nth(b, 4, t))
                    v.tensor_scalar(xbuf[t % 2][:, :], xbuf[t % 2][:, :], xr[:, 0:1], None, ALU.mult
                                    ).then_inc(S["s_xn"], 1)
                    for h in range(2):
                        v.wait_ge(S["s_xH"], nth(b, 8, 2 * t + h))
                        bank = (sbk, ptb)[h]
                        for k in range(4):
                            kk, cols = 4 * h + k, slice(t * P, (t + 1) * P)
                            i = v.scalar_tensor_tensor(out=hTL[:, kk, cols], in0=bank[:, k * P:(k + 1) * P],
                                                       scalar=ngain[:, kk:kk + 1], in1=hTH[:, kk, cols].bitcast(F32),
                                                       op0=ALU.mult, op1=ALU.subtract)
                        i.then_inc(S["s_xL"], 1)
                with v.Fori(0, NU) as u:
                    n = b * NU + u
                    link_at["s_dve"] = [0, n * UNIT_LINKS]
                    carry_in(n, u)
                    qkv(n, u, 0)
                    qkv(n, u, 1)
                    qkv(n, u, 2); tql(n, 0)
                    qkv(n, u, 3); tql(n, 1)
                    tql(n, 2); part1(n, 0); agg(n, 0); part2(n, 0)
                    tql(n, 3); part1(n, 1); agg(n, 1); part2(n, 1)
                    ptl(n, 0); rq_decay(n); part1(n, 2); rql(n); part2(n, 2)
                    ptl(n, 1); part1(n, 3); rkl(n); mix(n, 0); mixl(n, 0); part2(n, 3); rl(n, 0)
                    ptl(n, 2); rvg(n, 0); mix(n, 1); kw_am(n, 0); mixl(n, 1); kwl_al(n, 0)
                    ptl(n, 3); rvg(n, 1); mix(n, 2); rupd(n, 0); kw_am(n, 1); mixl(n, 2); rl(n, 1); kwl_al(n, 1)
                    gn(n, 0)
                    rvg(n, 2); mix(n, 3); rupd(n, 1); kw_am(n, 2); mixl(n, 3); rl(n, 2); kwl_al(n, 2); gn(n, 1)
                    mtl(n, 0)
                    rvg(n, 3); rupd(n, 2); kw_am(n, 3); rl(n, 3); kwl_al(n, 3); gn(n, 2); mtl(n, 1)
                    v.tensor_copy(kcar[:, bass.ds(u, 1), 0].rearrange("p o c -> p (o c)"), kHH[:, BLK:BLK + CHUNK].bitcast(F32))
                    v.tensor_copy(kcar[:, bass.ds(u, 1), 1].rearrange("p o c -> p (o c)"), kLL[:, BLK:BLK + CHUNK].bitcast(F32)
                                  ).then_inc(S["s_carry"], 1)
                    add(n, b, 0)
                    add(n, b, 1); rupd(n, 3, u)
                    add(n, b, 2); gn(n, 3); mtl(n, 2)
                    add(n, b, 3); mtl(n, 3)
                    for i in range(4, 8):
                        add(n, b, i)
                    assert link_at["s_dve"][0] == UNIT_LINKS, link_at

        @block.tensor
        def _(pe):
            pe.sem_inc(S["s_job"], CREDIT_JOB)
            pe.wait_ge(S["s_ident"], 96)

            def mm3(o, pairs):
                last = len(pairs) - 1
                for i, ((lh, ll), (rh_, rl_)) in enumerate(pairs):
                    pe.matmul(o, lh, rh_, start=i == 0, stop=False)
                    pe.matmul(o, lh, rl_, start=False, stop=False)
                    m = pe.matmul(o, ll, rh_, start=False, stop=i == last)
                return m

            def bank_free(n, j):
                if j < 2:
                    pe.wait_ge(S["s_acc"], n * 8 + (6 + j + 1))
                elif j < 6:
                    pe.wait_ge(S["s_raw"], nth(n, 4, j - 2))
                elif j < 8:
                    pe.wait_ge(S["s_gate"], nth(n, 2, j - 6))
                elif j == 8:
                    pe.wait_ge(S["s_qpr"], nth(n, 1, 0))
                elif j == 9:
                    pe.wait_ge(S["s_rkl"], nth(n, 1, 0))
                elif j < 14:
                    pe.wait_ge(S["s_rvg"], nth(n, 4, j - 10))
                else:
                    pe.wait_ge(S["s_acc"], nth(n, 8, j - 14) + CREDIT_ACC)

            def job(n, b, j):
                bank_free(n, j)
                if j == 0:
                    pe.wait_ge(S["s_xL"], 8 * b + 8)
                if j < J_OUT:
                    p = 0 if j < J_AG else 1 if j < J_RVG else 2
                    W, L = wH[p % 2], wL[p % 2]
                    pairs = []
                    for k in range(KT):
                        if j < J_AG or j >= J_RVG:
                            t = j if j < J_AG else j - J_RVG
                            cols = slice(t * P, (t + 1) * P)
                            w = W_WIDTH[p]
                            o = jb[j % 2][:, 0:w]
                            pairs.append(((hTH[:, k, cols], hTL[:, k, cols]), (W[:, k, 0:w], L[:, k, 0:w])))
                        else:
                            f = slice((j - J_AG) * P, (j - J_AG + 1) * P)
                            o = jb[j % 2][:, :]
                            pairs.append(((W[:, k, f], L[:, k, f]), (hTH[:, k, :], hTL[:, k, :])))
                    first = j in (J_QKV, J_AG, J_RVG)
                else:
                    t, h = (j - J_OUT) // 2, (j - J_OUT) % 2
                    p, W, L = 3, wH[1], wL[1]
                    if h == 0:
                        pe.wait_ge(S["s_mixl"], nth(n, 4, t))
                        pe.wait_ge(S["s_mtl"], nth(n, 4, t))
                    cols = slice(t * P, (t + 1) * P)
                    o = jb[j % 2][:, :]
                    pairs = [((mxH[:, k, cols], mxL[:, k, cols]), (W[:, 4 * h + k, :], L[:, 4 * h + k, :]))
                             for k in range(4)]
                    first = t == 0
                last = len(pairs) - 1
                for i, ((lh, ll), (rh_, rl_)) in enumerate(pairs):
                    if first:
                        s = i if p < 3 else 4 * h + i
                        pe.wait_ge(S["s_wl"], nth(n, 32, 8 * p + s) + CREDIT_WL)
                    pe.matmul(o, lh, rh_, start=i == 0, stop=False)
                    pe.matmul(o, lh, rl_, start=False, stop=False)
                    m = pe.matmul(o, ll, rh_, start=False, stop=i == last)
                m.then_inc(S["s_job"], 1)

            def TQ(n, t):
                pe.wait_ge(S["s_qn"], nth(n, 4, t))
                if t >= 1:
                    pe.wait_ge(S["s_tql"], nth(n, 4, t - 1))
                for c in range(3):
                    m = pe.transpose(tr[:, c * P:(c + 1) * P], qn[:, t % 2, c * P:(c + 1) * P], ident[:, :])
                m.then_inc(S["s_tq"], 1)

            def S_(n, t):
                pe.wait_ge(S["s_tql"], nth(n, 4, t))
                if t == 0:
                    pe.wait_ge(S["s_carin"], nth(n, 1, 0))
                else:
                    pe.wait_ge(S["s_x"], nth(n, 4, t - 1))
                for pos in range(2):
                    par = pos if t == 0 else 1 - pos
                    own = CHUNK + t * P
                    for hp in range(2):
                        q = qS[:, t, 2 * hp + par]
                        at = pos * 256 + hp * P
                        if par == 1:
                            runs = [(at, P, own)]
                        else:
                            runs = [(at, CHUNK, own), (at + CHUNK, CHUNK, own - CHUNK)]
                        for to, w, col in runs:
                            pe.matmul(sbk[:, to:to + w], q, kHH[:, col:col + w], start=True, stop=False)
                            m = pe.matmul(sbk[:, to:to + w], q, kLL[:, col:col + w], start=False, stop=True)
                m.then_inc(S["s_s"], 1)

            def PT(n, t):
                pe.wait_ge(S["s_pn"], nth(n, 4, t))
                if t >= 1:
                    pe.wait_ge(S["s_ptl"], nth(n, 4, t - 1))
                for i in range(4):
                    at = (t % 2) * 512 + i * P
                    m = pe.transpose(ptb[:, i * P:(i + 1) * P], sx[:, at:at + P], ident[:, :])
                m.then_inc(S["s_pt"], 1)

            def PV(n, t):
                pe.wait_ge(S["s_ptl"], nth(n, 4, t))
                if t >= 1:
                    pe.wait_ge(S["s_mixr"], nth(n, 4, t - 1))
                for pos in range(2):
                    par = pos if t == 0 else 1 - pos
                    vh, vl = (voH[:, t], voL[:, t]) if par else (veH[:, t], veL[:, t])
                    o = ob[0:64, :].rearrange("p (r c q) -> p r c q", c=2, q=64)[:, :, par]
                    cols = slice(pos * 256, pos * 256 + 256)
                    ph = pTH[:, cols].rearrange("p (r q) -> p r q", q=64)
                    pl = pTL[:, cols].rearrange("p (r q) -> p r q", q=64)
                    m = mm3(o, [((vh, vl), (ph, pl))])
                m.then_inc(S["s_pv"], 1)

            def KT_(n, t):
                if t == 0:
                    pe.wait_ge(S["s_rkh"], nth(n, 1, 0))
                    pe.wait_ge(S["s_tql"], nth(n, 4, 3))
                elif t < 3:
                    pe.wait_ge(S["s_kw"], nth(n, 4, t - 1))
                else:
                    pe.wait_ge(S["s_mtl"], nth(n, 4, 0))
                pe.transpose(tr[:, 0:P], kr[:, t * P:(t + 1) * P], ident[:, :]).then_inc(S["s_kt"], 1)

            def A(n, t):
                if t == 0:
                    pe.wait_ge(S["s_rql"], nth(n, 1, 0))
                    pe.wait_ge(S["s_rkl"], nth(n, 1, 0))
                else:
                    pe.wait_ge(S["s_am"], nth(n, 4, t - 1))
                cols = slice(t * P, (t + 1) * P)
                m = mm3(ab[:, 0:256].rearrange("p (a i) -> p a i", a=2),
                        [((rkH[:, cols], rkL[:, cols]), (rqH[:, :, cols], rqL[:, :, cols]))])
                m.then_inc(S["s_a"], 1)

            def I(n, t):
                pe.wait_ge(S["s_rl"], nth(n, 4, t))
                pe.wait_ge(S["s_kwl"], nth(n, 4, t))
                pe.wait_ge(S["s_al"], nth(n, 4, t))
                pe.wait_ge(S["s_rvg"], nth(n, 4, t))
                if t >= 1:
                    pe.wait_ge(S["s_oc"], nth(n, 4, t - 1))
                cols = slice(t * P, (t + 1) * P)
                for a in range(2):
                    e = slice(a * P, (a + 1) * P)
                    mm3(ro[:, e], [((rqH[:, a, cols], rqL[:, a, cols]), (rH[:, :], rL[:, :])),
                                   ((aH[:, e], aL[:, e]), (rvH[:, t % 2, e], rvL[:, t % 2, e]))])
                m = mm3(ro[:, 256:512], [((kwH[:, :], kwL[:, :]), (rvH[:, t % 2], rvL[:, t % 2]))])
                m.then_inc(S["s_i"], 1)

            def MT(n, t):
                pe.wait_ge(S["s_mr"], nth(n, 4, t))
                if t < 2:
                    pe.wait_ge(S["s_kw"], nth(n, 4, t + 2))
                else:
                    pe.wait_ge(S["s_mtl"], nth(n, 4, t - 1))
                for h in range(2):
                    m = pe.transpose(tr[:, h * P:(h + 1) * P], mr[:, h], ident[:, :])
                m.then_inc(S["s_mt"], 1)

            steps = {"TQ": TQ, "S": S_, "PT": PT, "PV": PV, "KT": KT_, "A": A, "I": I, "MT": MT}

            with pe.Fori(0, NB) as b:
                for t in range(NT):
                    pe.wait_ge(S["s_xn"], nth(b, 4, t))
                    for h in range(2):
                        if t >= 1:
                            pe.wait_ge(S["s_xL"], nth(b, 8, 2 * (t - 1) + h))
                        bank = (sbk, ptb)[h]
                        for k in range(4):
                            kk = 4 * h + k
                            m = pe.transpose(bank[:, k * P:(k + 1) * P], xbuf[t % 2][:, kk * P:(kk + 1) * P], ident[:, :])
                        m.then_inc(S["s_xT"], 1)
                with pe.Fori(0, NU) as u:
                    n = b * NU + u
                    for j in range(JOBS):
                        for what, t in STEPS.get(j, ()):
                            steps[what](n, t)
                        job(n, b, j)


_OUT_SHAPE = (1, SEQ, DM)


def kernel(**inputs):
    import numpy as np
    import concourse.bacc as bacc
    from concourse.bass_utils import run_bass_kernel_spmd as run

    f32 = np.float32
    slopes = (2.0 ** (-8.0 * (np.arange(HEADS) + 1.0) / HEADS)).astype(f32)
    q = np.arange(CHUNK)[:, None]
    ki = np.arange(2 * CHUNK)[None, :]
    dist = np.abs(q + CHUNK - ki).astype(f32)
    even = np.concatenate([dist[:, CHUNK:], dist[:, :CHUNK]], axis=1)
    c_bias = np.zeros((KVH, P, 512), f32)
    c_bias0 = np.zeros((NB, KVH, P, 256), f32)
    for g in range(KVH):
        for hp in range(2):
            for a in range(2):
                s = -slopes[4 * g + 2 * hp + a]
                rows = slice(64 * a, 64 * a + 64)
                c_bias[g, rows, hp * P:(hp + 1) * P] = s * dist
                c_bias[g, rows, 256 + hp * P:256 + (hp + 1) * P] = s * even
                c_bias0[:, g, rows, hp * P:(hp + 1) * P] = s * even
                c_bias0[0, g, rows, hp * P + CHUNK:(hp + 1) * P] = -1e30
    c_ret = np.zeros((NU, P, 513), f32)
    i = np.arange(P)
    scale = HD ** -0.5
    for h in range(RET_HEADS):
        u, a = h // 2, h % 2
        g = 1.0 - 2.0 ** (-5.0 - h)
        di = g ** np.abs(i[None, :] - i[:, None]) * (i[:, None] // CHUNK <= i[None, :] // CHUNK)
        c_ret[u, :, a * P:(a + 1) * P] = scale * di * g ** (-(i[None, :] + 1.0))
        rows = slice(64 * a, 64 * a + 64)
        c_ret[u, rows, 256:384] = g ** (i[None, :] + 1.0)
        c_ret[u, :, 384 + 64 * a:384 + 64 * a + 64] = (scale * g ** (127.0 - i))[:, None]
        c_ret[u, rows, 512] = g ** 128.0

    nc = bacc.Bacc("TRN2", target_bir_lowering=False, num_devices=1, dynamic_dma_scratch_size=8192)
    names = ("x", "norm_gain", "w_in", "q_norm_gain", "k_norm_gain", "sink_logits", "ret_norm_gain", "w_out")
    arrays = {f"{n}_dram": np.ascontiguousarray(inputs[n]) for n in names}
    arrays.update(c_bias0_dram=c_bias0, c_bias_dram=c_bias, c_ret_dram=c_ret, c_ident_dram=np.eye(P, dtype=f32))
    args = [nc.dram_tensor(n, a.shape, F32, kind="ExternalInput").ap() for n, a in arrays.items()]
    out = nc.dram_tensor("out_dram", _OUT_SHAPE, F32, kind="ExternalOutput").ap()
    build(nc, *args, out)
    r = run(nc, [arrays], core_ids=[0])
    return r.results[0]["out_dram"]
```

```python
from contextlib import ExitStack

import concourse.bass as bass
from concourse import mybir

F32 = mybir.dt.float32
F32R = mybir.dt.float32r
ALU = mybir.AluOpType
ACT = mybir.ActivationFunctionType
AX = mybir.AxisListType

P = 128
SEQ, DM = 2048, 1024
CHUNK = 64
HD = 64
HEADS, KVH = 16, 4
RET_HEADS, RV = 8, 128
EPS = 1e-6
BLK = 512
NB = SEQ // BLK
NT = BLK // P
KT = DM // P
NU = KVH
C_AQ, C_AK, C_AV, C_AG, C_RQ, C_RK, C_RV, C_RG = 0, 1024, 1280, 1536, 2560, 3072, 3584, 4608
D_ATTN = 1024

J_QKV, J_AG, J_RQ, J_RK, J_RVG, J_OUT, JOBS = 0, 4, 6, 7, 8, 12, 20
W_SUBS = 8
W_PANELS = 4
W_WIDTH = [384, 512, 512, 512]
W_DMAS = [3, 3, 2, 1]
STEPS = {
    3: [("TQ", 0)], 4: [("TQ", 1)], 5: [("TQ", 2), ("S", 0)], 6: [("TQ", 3), ("S", 1)],
    7: [("PT", 0), ("S", 2)], 8: [("PT", 1), ("PV", 0), ("S", 3)],
    9: [("PT", 2), ("PV", 1), ("KT", 0), ("A", 0)],
    10: [("PT", 3), ("PV", 2), ("I", 0), ("KT", 1), ("A", 1)],
    11: [("PV", 3), ("I", 1), ("KT", 2), ("A", 2), ("MT", 0)],
    12: [("I", 2), ("KT", 3), ("A", 3)],
    13: [("I", 3), ("MT", 1)], 15: [("MT", 2)], 17: [("MT", 3)],
}
X_STEPS = {15: 0, 16: 1, 18: 2, 20: 3}
STAGES = 4
CREDIT_JOB, CREDIT_ACC, CREDIT_SAVE, CREDIT_UPD, CREDIT_WL = JOBS, 2 * NT, 1, NT, 32


def nth(n, per_unit, j):
    return n * per_unit + (j + 1)


def build(nc, x, norm_gain, w_in, q_gain, k_gain, sinks, ret_gain, w_out, c_bias0, c_bias, c_ret, c_ident, out):
    w_in_v = w_in.rearrange("(k p) n -> p k n", p=P)
    w_out_v = w_out.rearrange("(k p) n -> p k n", p=P)
    sinks_v = sinks.rearrange("(h a) -> a h", a=2)

    with ExitStack() as ctx:
        def sb(name, shape, dt=F32):
            return ctx.enter_context(nc.sbuf_tensor(name, shape, dt))

        def pb(name):
            return ctx.enter_context(nc.psum_tensor(name, [P, 512], F32))

        def sem(name):
            return ctx.enter_context(nc.semaphore(name))

        hTH, hTL = sb("hTH", [P, KT, BLK], F32R), sb("hTL", [P, KT, BLK], F32R)
        wH = [sb(f"wH{i}", [P, W_SUBS, 512], F32R) for i in range(2)]
        wL = [sb(f"wL{i}", [P, W_SUBS, 512], F32R) for i in range(2)]
        stage = sb("stage", [P, STAGES, 2, 512])
        acc = sb("acc", [P, NT, DM])
        mxH, mxL = sb("mxH", [P, 4, BLK], F32R), sb("mxL", [P, 4, BLK], F32R)
        gate = sb("gate", [P, 2 * BLK])
        sx = sb("sx", [P, 2 * BLK])
        xbuf = [gate, sx]
        th = sb("th", [P, BLK])
        raw = sb("raw", [P, 2, 384])
        qn = sb("qn", [P, 2, 384])
        qS = sb("qS", [P, NT, 4, P], F32R)
        kHH, kLL = sb("kHH", [P, CHUNK + BLK], F32R), sb("kLL", [P, CHUNK + BLK], F32R)
        voH, voL = sb("voH", [P, NT, HD], F32R), sb("voL", [P, NT, HD], F32R)
        veH, veL = sb("veH", [P, NT, HD], F32R), sb("veL", [P, NT, HD], F32R)
        kcar = sb("kcar", [P, NU, 2, CHUNK], F32R)
        vcar = sb("vcar", [P, NU, 2, HD], F32R)
        pTH, pTL = sb("pTH", [P, 512], F32R), sb("pTL", [P, 512], F32R)
        mixr = sb("mixr", [P, 2, P])
        bias = sb("bias", [P, 768])
        sink, nsink = sb("sink", [P, 2]), sb("nsink", [P, 2])
        m4, nm4, d4, den, es, rc = (sb(n_, [P, 4]) for n_ in ("m4", "nm4", "d4", "den", "es", "rc"))
        ss, ms, rstd = sb("ss", [P, 5]), sb("ms", [P, 5]), sb("rstd", [P, 5])
        mhalf = sb("mhalf", [P, 8])
        rqH, rqL = sb("rqH", [P, 2, BLK], F32R), sb("rqL", [P, 2, BLK], F32R)
        rkH, rkL = sb("rkH", [P, BLK], F32R), sb("rkL", [P, BLK], F32R)
        kr = sb("kr", [P, BLK])
        rvH, rvL = sb("rvH", [P, 2, 2 * RV], F32R), sb("rvL", [P, 2, 2 * RV], F32R)
        gg = sb("gg", [P, 2, 2 * RV])
        kwr, kwH, kwL = sb("kwr", [P, P]), sb("kwH", [P, P], F32R), sb("kwL", [P, P], F32R)
        amr, aH, aL = sb("amr", [P, 2 * P]), sb("aH", [P, 2 * P], F32R), sb("aL", [P, 2 * P], F32R)
        rst = sb("rst", [P, NU, RV])
        rcur, rH, rL = sb("rcur", [P, RV]), sb("rH", [P, RV], F32R), sb("rL", [P, RV], F32R)
        oraw, mr = sb("oraw", [P, 2, RV]), sb("mr", [P, 2, RV])
        st, mv, ve, grs = sb("st", [P, 2, 6]), sb("mv", [P, 2, 2]), sb("ve", [P, 2]), sb("grs", [P, 2])
        cret = sb("cret", [P, 513])
        cD, cwq, cwk, cg = cret[:, 0:256], cret[:, 256:384], cret[:, 384:512], cret[:, 512:513]
        gain = sb("gain", [P, 2 * RV])
        ident = sb("ident", [P, P])
        ngain = sb("ngain", [P, KT])
        qkg = sb("qkg", [P, 2])
        xss, xms, xr = sb("xss", [P, 2]), sb("xms", [P, 2]), sb("xr", [P, 1])

        jb = [pb("jb0"), pb("jb1")]
        tr, sbk, ptb, ob, ab, ro = pb("tr"), pb("sbk"), pb("ptb"), pb("ob"), pb("ab"), pb("ro")

        names = """s_ident s_mhalf s_zero s_x0 s_x1 s_xsq s_xms s_xr s_xn s_xT s_xH s_xL s_accin s_store
            s_w0 s_w1 s_w2 s_w3 s_wh s_wl s_job s_cattn s_cret s_raw s_sq s_voh s_ms s_rstd s_qn s_tq s_tqh s_tql
            s_s s_x s_nm s_exp s_pn s_pt s_pth s_ptl s_pv s_mixr s_mixh s_mixl s_agt s_gate
            s_qpr s_rqh s_rql s_rkh s_rkl s_rvt s_rvg s_kt s_kw s_kwh s_kwl s_a s_am s_ah s_al
            s_i s_rupd s_oc s_rh s_rl s_rcur s_var s_grs s_mr s_mt s_mth s_mtl s_acc s_nsink s_carin s_carry
            s_dve s_dvex""".split()
        S = {name: sem(name) for name in names}
        s_x = [S["s_x0"], S["s_x1"]]
        s_w = [S["s_w0"], S["s_w1"], S["s_w2"], S["s_w3"]]
        xbanks = ((sbk, ptb), (ob, ab))
        block = ctx.enter_context(nc.Block())

        @block.sync
        def _(sp):
            for dst, src in ((ident[:, :], c_ident), (ngain[:, :], norm_gain.rearrange("(k p) -> p k", p=P))):
                sp.dma_start(dst, src, allow_slow_non_contiguous=True).then_inc(S["s_ident"], 16)
            for half in range(2):
                rows = slice(half * HD, half * HD + HD)
                sp.dma_start(qkg[rows, 0:1], q_gain.rearrange("(d o) -> d o", o=1)).then_inc(S["s_ident"], 16)
                sp.dma_start(qkg[rows, 1:2], k_gain.rearrange("(d o) -> d o", o=1)).then_inc(S["s_ident"], 16)

            def panel(n, u, p):
                for c in range(4):
                    sp.wait_ge(S["s_wl"], nth(n, 32, 8 * (p - 1) + 2 * c + 1) + CREDIT_WL)
                    dst, done = stage[:, c], s_w[c]
                    if p < 3:
                        strips = (((0, 256, C_AQ), (256, 64, C_AK), (320, 64, C_AV)),
                                  ((0, 256, C_AG), (256, 128, C_RQ), (384, 128, C_RK)),
                                  ((0, 256, C_RV), (256, 256, C_RG)))[p]
                        for at, w, col in strips:
                            sp.dma_start(dst[:, :, at:at + w],
                                         w_in_v[:, 2 * c:2 * c + 2, bass.ds(u * w + col, w)]).then_inc(done, 16)
                    else:
                        base = (c % 2) * KT
                        sp.dma_start(dst[:, :, :], w_out_v[:, bass.ds(u * 2 + base, 2),
                                                           (c // 2) * 512:(c // 2 + 1) * 512]).then_inc(done, 16)

            def x_tile(b, t):
                if t < 2:
                    sp.wait_ge(S["s_carry"], NU * b + 1)
                else:
                    sp.wait_ge(S["s_xT"], nth(b, 4, t - 2))
                sp.dma_start(xbuf[t % 2][:, :], x[0, bass.ds(b * BLK + t * P, P), :]).then_inc(s_x[t % 2], 16)

            def rest(b, u, first=False):
                n = b * NU + u
                sp.wait_ge(S["s_carry"], n + 1)
                sp.dma_start(bias[:, 0:256], c_bias0[b, u]).then_inc(S["s_cattn"], 16)
                sp.dma_start(bias[:, 256:768], c_bias[u]).then_inc(S["s_cattn"], 16)
                for a in range(2):
                    sp.dma_start(sink[a * 64:a * 64 + 64, :],
                                 sinks_v[a, bass.ds(u * 2, 2)].partition_broadcast(64),
                                 allow_slow_non_contiguous=True).then_inc(S["s_cattn"], 16)
                sp.wait_ge(S["s_var"], 4 * n + CREDIT_UPD)
                sp.dma_start(cret[:, :], c_ret[u]).then_inc(S["s_cret"], 16)
                sp.dma_start(gain[:, :], ret_gain[bass.ds(u * 256, 256)].partition_broadcast(P)).then_inc(S["s_cret"], 16)
                panel(n, u, 1)
                if first:
                    sp.wait_ge(S["s_store"], 16 * b + 16)
                    sp.dma_start(acc[:, :, :], x[0, bass.ds(b * BLK, BLK), :].rearrange("(t p) d -> p t d", p=P)
                                 ).then_inc(S["s_accin"], 16)
                panel(n, u, 2)
                panel(n, u, 3)

            def store(b):
                sp.wait_ge(S["s_acc"], b * 32 + (32 + CREDIT_ACC))
                sp.dma_start(out[0, bass.ds(b * BLK, BLK), :].rearrange("(t p) d -> p t d", p=P), acc[:, :, :]
                             ).then_inc(S["s_store"], 16)

            def units(b):
                rest(b, 0, first=True)
                panel(b * NU + 1, 1, 0)
                with sp.Fori(1, NU - 1) as u:
                    rest(b, u)
                    panel(b * NU + u + 1, u + 1, 0)
                rest(b, NU - 1)

            for t in range(NT):
                if t == 2:
                    panel(0, 0, 0)
                x_tile(0, t)
            with sp.Fori(0, NB - 1) as b:
                units(b)
                x_tile(b + 1, 0)
                x_tile(b + 1, 1)
                panel((b + 1) * NU, 0, 0)
                x_tile(b + 1, 2)
                x_tile(b + 1, 3)
                store(b)
            units(NB - 1)
            store(NB - 1)
            sp.wait_ge(S["s_store"], 16 * (NB + 1))

        @block.gpsimd
        def _(pool):
            pool.memset(mhalf[:, :], -0.5).then_inc(S["s_mhalf"], 1)
            pool.sem_inc(S["s_wl"], CREDIT_WL)
            pool.wait_ge(S["s_mhalf"], 1)

            def wl(n, p, subs):
                for s in subs:
                    pool.wait_ge(S["s_wh"], nth(n, 32, 8 * p + s))
                    w = W_WIDTH[p]
                    pool.tensor_tensor(wL[p % 2][:, s, 0:w], stage[:, s // 2, s % 2, 0:w],
                                       wH[p % 2][:, s, 0:w].bitcast(F32), ALU.subtract).then_inc(S["s_wl"], 1)

            def rpow(n, t):
                pool.wait_ge(S["s_ms"], nth(n, 4, t))
                pool.tensor_tensor(rstd[:, :], ms[:, :], mhalf[:, 0:5], ALU.pow).then_inc(S["s_rstd"], 1)

            def gpow(n, t):
                pool.wait_ge(S["s_var"], nth(n, 4, t) + CREDIT_UPD)
                pool.tensor_tensor(grs[:, :], ve[:, :], mhalf[:, 0:2], ALU.pow).then_inc(S["s_grs"], 1)

            def xpow(b, t):
                pool.wait_ge(S["s_xms"], nth(b, 4, t))
                pool.tensor_tensor(xr[:, :], xms[:, 1:2], mhalf[:, 0:1], ALU.pow).then_inc(S["s_xr"], 1)

            def unit(b, u, nxt, x_next):
                n = b * NU + u
                rpow(n, 0); wl(n, 1, (0, 1, 2))
                rpow(n, 1); wl(n, 1, (3, 4, 5))
                rpow(n, 2); wl(n, 1, (6, 7))
                rpow(n, 3); wl(n, 2, range(8))
                wl(n, 3, range(0, 6))
                gpow(n, 0); wl(n, 3, (6, 7))
                gpow(n, 1); gpow(n, 2)
                if nxt:
                    wl(n + 1, 0, (0, 1))
                gpow(n, 3)
                for t in range(NT):
                    if x_next:
                        xpow(b + 1, t)
                    if nxt and t < 3:
                        wl(n + 1, 0, (2 * t + 2, 2 * t + 3))

            for t in range(NT):
                xpow(0, t)
                wl(0, 0, (2 * t, 2 * t + 1))
            with pool.Fori(0, NB - 1) as b:
                with pool.Fori(0, NU - 1) as u:
                    unit(b, u, True, False)
                unit(b, NU - 1, True, True)
            with pool.Fori(0, NU - 1) as u:
                unit(NB - 1, u, True, False)
            unit(NB - 1, NU - 1, False, False)

        @block.scalar
        def _(act):
            act.wait_ge(S["s_ident"], 96)

            def wh(n, p, subs):
                for s in subs:
                    c = s // 2
                    if s == subs[0]:
                        last = {0: J_OUT - 1 - JOBS, 1: JOBS - 1 - JOBS, 2: J_AG - 1, 3: J_RK}[p]
                        act.wait_ge(S["s_job"], nth(n, JOBS, last) + CREDIT_JOB)
                    if s % 2 == 0 or s == subs[0]:
                        done = sum(W_DMAS[:p + 1])
                        act.wait_ge(s_w[c], n * (16 * sum(W_DMAS)) + 16 * done)
                    w = W_WIDTH[p]
                    act.activation(wH[p % 2][:, s, 0:w], stage[:, c, s % 2, 0:w], ACT.Copy).then_inc(S["s_wh"], 1)

            def qkv(n, t):
                act.wait_ge(S["s_job"], nth(n, JOBS, J_QKV + t) + CREDIT_JOB)
                if t >= 2:
                    act.wait_ge(S["s_qn"], nth(n, 4, t - 2))
                act.activation(raw[:, t % 2], jb[t % 2][:, 0:384], ACT.Copy).then_inc(S["s_raw"], 1)
                act.wait_ge(S["s_raw"], nth(n, 4, t))
                if t >= 1:
                    act.wait_ge(S["s_ms"], nth(n, 4, t - 1))
                act.activation(th[:, 0:320], raw[:, t % 2, 0:320], ACT.Square).then_inc(S["s_sq"], 1)
                act.activation(voH[:, t], raw[:, t % 2, 320:384], ACT.Copy).then_inc(S["s_voh"], 1)

            def tqh(n, t):
                act.wait_ge(S["s_tq"], nth(n, 4, t))
                for a in range(2):
                    rows = slice(a * 64, a * 64 + 64)
                    act.activation(qS[rows, t, :, a * 64:a * 64 + 64],
                                   tr[rows, 0:256].rearrange("p (c q) -> p c q", q=64), ACT.Copy, scale=qkg[rows, 0:1])
                act.activation(kHH[:, CHUNK + t * P:CHUNK + (t + 1) * P], tr[:, 256:384], ACT.Copy,
                               scale=qkg[:, 1:2]).then_inc(S["s_tqh"], 1)

            def ag(n, i):
                act.wait_ge(S["s_job"], nth(n, JOBS, J_AG + i) + CREDIT_JOB)
                if i == 0:
                    act.wait_ge(S["s_ms"], nth(n, 4, 3))
                else:
                    act.wait_ge(S["s_gate"], nth(n, 2, 0))
                act.activation(th[:, :], jb[i % 2][:, :], ACT.Tanh, scale=0.5).then_inc(S["s_agt"], 1)

            def exps(n, t):
                act.wait_ge(S["s_nm"], nth(n, 4, t))
                for i in range(4):
                    v = sx[:, (t % 2) * 512 + i * P:(t % 2) * 512 + (i + 1) * P]
                    act.activation(v, v, ACT.Exp, bias=nm4[:, i:i + 1], accum_out=den[:, i:i + 1])
                act.activation(es[:, :], d4[:, :], ACT.Exp).then_inc(S["s_exp"], 1)

            def pth(n, t):
                act.wait_ge(S["s_pt"], nth(n, 4, t))
                if t >= 1:
                    act.wait_ge(S["s_pv"], nth(n, 4, t - 1))
                act.activation(pTH[:, :], ptb[:, :], ACT.Copy).then_inc(S["s_pth"], 1)

            def rqh(n):
                act.wait_ge(S["s_qpr"], nth(n, 1, 0))
                for a in range(2):
                    rows = slice(a * 64, a * 64 + 64)
                    i = act.activation(rqH[rows, a], th[rows, :], ACT.Copy)
                i.then_inc(S["s_rqh"], 1)

            def rk(n):
                act.wait_ge(S["s_job"], nth(n, JOBS, J_RK) + CREDIT_JOB)
                act.activation(kr[:, :], jb[1][:, :], ACT.Copy)
                act.activation(rkH[:, :], jb[1][:, :], ACT.Copy).then_inc(S["s_rkh"], 1)

            def rvg(n, t):
                act.wait_ge(S["s_job"], nth(n, JOBS, J_RVG + t) + CREDIT_JOB)
                if t >= 2:
                    act.wait_ge(S["s_i"], nth(n, 4, t - 2))
                act.activation(rvH[:, t % 2], jb[t % 2][:, 0:256], ACT.Copy)
                if t == 0:
                    act.wait_ge(S["s_rql"], nth(n, 1, 0))
                else:
                    act.wait_ge(S["s_rvg"], nth(n, 4, t - 1))
                act.activation(th[:, 0:256], jb[t % 2][:, 256:512], ACT.Tanh, scale=0.5).then_inc(S["s_rvt"], 1)

            def mixh(n, t):
                act.wait_ge(S["s_mixr"], nth(n, 4, t))
                act.activation(mxH[:, 0:2, t * P:(t + 1) * P], mixr[:, :, :], ACT.Copy).then_inc(S["s_mixh"], 1)

            def kwh_ah(n, t):
                act.wait_ge(S["s_kw"], nth(n, 4, t))
                if t >= 1:
                    act.wait_ge(S["s_i"], nth(n, 4, t - 1))
                act.activation(kwH[:, :], kwr[:, :], ACT.Copy).then_inc(S["s_kwh"], 1)
                act.wait_ge(S["s_am"], nth(n, 4, t))
                act.activation(aH[:, :], amr[:, :], ACT.Copy).then_inc(S["s_ah"], 1)

            def rh(n, t):
                if t == 0:
                    act.wait_ge(S["s_rcur"], nth(n, 1, 0))
                else:
                    act.wait_ge(S["s_rupd"], nth(n, 4, t - 1) + CREDIT_UPD)
                act.activation(rH[:, :], rcur[:, :], ACT.Copy).then_inc(S["s_rh"], 1)

            def ocopy(n, t):
                act.wait_ge(S["s_rupd"], nth(n, 4, t) + CREDIT_UPD)
                if t >= 1:
                    act.wait_ge(S["s_mr"], nth(n, 4, t - 1))
                act.activation(oraw[:, :, :], ro[:, 0:256].rearrange("p (h e) -> p h e", h=2), ACT.Copy
                               ).then_inc(S["s_oc"], 1)

            def mth(n, t):
                act.wait_ge(S["s_mt"], nth(n, 4, t))
                act.activation(mxH[:, 2:4, t * P:(t + 1) * P], tr[:, 0:256].rearrange("p (h q) -> p h q", h=2),
                               ACT.Copy).then_inc(S["s_mth"], 1)

            def xsq(b, t):
                act.wait_ge(s_x[t % 2], b * 32 + 16 * (t // 2 + 1))
                if t >= 1:
                    act.wait_ge(S["s_xms"], nth(b, 4, t - 1))
                for h in range(2):
                    i = act.activation((th, kr)[h][:, :], xbuf[t % 2][:, h * 512:(h + 1) * 512], ACT.Square,
                                       accum_out=xss[:, h:h + 1])
                i.then_inc(S["s_xsq"], 1)

            def xh(b, t):
                act.wait_ge(S["s_xT"], nth(b, 4, t))
                for h in range(2):
                    for k in range(4):
                        i = act.activation(hTH[:, 4 * h + k, t * P:(t + 1) * P], xbanks[t % 2][h][:, k * P:(k + 1) * P],
                                           ACT.Copy, scale=ngain[:, 4 * h + k:4 * h + k + 1])
                    i.then_inc(S["s_xH"], 1)

            def unit(b, u, nxt, x_next):
                n = b * NU + u
                w = lambda *subs: wh(n + 1, 0, list(subs)) if nxt else None
                qkv(n, 0); wh(n, 1, [0, 1, 2])
                qkv(n, 1); wh(n, 1, [3, 4, 5])
                tqh(n, 0); qkv(n, 2); wh(n, 1, [6, 7])
                tqh(n, 1); qkv(n, 3); wh(n, 2, [0, 1])
                tqh(n, 2); ag(n, 0); wh(n, 2, [2, 3]); exps(n, 0)
                tqh(n, 3); ag(n, 1); wh(n, 2, [4, 5]); exps(n, 1)
                pth(n, 0); rqh(n); wh(n, 2, [6, 7]); exps(n, 2)
                pth(n, 1); rk(n); mixh(n, 0); wh(n, 3, [0, 1]); exps(n, 3); rh(n, 0)
                pth(n, 2); rvg(n, 0); mixh(n, 1); kwh_ah(n, 0); wh(n, 3, [2, 3])
                pth(n, 3); rvg(n, 1); mixh(n, 2); ocopy(n, 0); rh(n, 1); kwh_ah(n, 1); wh(n, 3, [4, 5])
                rvg(n, 2); mixh(n, 3); ocopy(n, 1); rh(n, 2); kwh_ah(n, 2); mth(n, 0); wh(n, 3, [6, 7])
                rvg(n, 3); ocopy(n, 2); rh(n, 3); kwh_ah(n, 3); w(0, 1)
                if x_next:
                    xsq(b + 1, 0)
                mth(n, 1); ocopy(n, 3)
                if x_next:
                    xsq(b + 1, 1)
                w(2, 3); mth(n, 2)
                if x_next:
                    xh(b + 1, 0); xsq(b + 1, 2); xh(b + 1, 1)
                w(4, 5); mth(n, 3)
                if x_next:
                    xsq(b + 1, 3); xh(b + 1, 2)
                w(6, 7)
                if x_next:
                    xh(b + 1, 3)

            for t in range(NT):
                xsq(0, t)
                if t >= 1:
                    xh(0, t - 1)
                wh(0, 0, [2 * t, 2 * t + 1])
            xh(0, NT - 1)
            with act.Fori(0, NB - 1) as b:
                with act.Fori(0, NU - 1) as u:
                    unit(b, u, True, False)
                unit(b, NU - 1, True, True)
            with act.Fori(0, NU - 1) as u:
                unit(NB - 1, u, True, False)
            unit(NB - 1, NU - 1, False, False)

        @block.vector
        def _(v):
            UNIT_LINKS = 36
            link_at = [0, 0]

            def link(ins):
                ins.then_inc(S["s_dve"], 1)
                link_at[0] += 1
                v.wait_ge(S["s_dve"], link_at[1] + link_at[0])

            def sub(out, a, h):
                return v.tensor_tensor(out, a, h.bitcast(F32), ALU.subtract)

            v.memset(rst[:, :, :], 0.0).then_inc(S["s_zero"], 1)
            v.memset(rqH[:, :, :].bitcast(F32), 0.0).then_inc(S["s_zero"], 1)
            v.memset(rqL[:, :, :].bitcast(F32), 0.0).then_inc(S["s_zero"], 1)
            v.memset(kcar[:, :, :, :].bitcast(F32), 0.0).then_inc(S["s_zero"], 1)
            v.memset(vcar[:, :, :, :].bitcast(F32), 0.0).then_inc(S["s_zero"], 1)
            v.sem_inc(S["s_acc"], CREDIT_ACC)
            v.sem_inc(S["s_carry"], CREDIT_SAVE)
            v.sem_inc(S["s_rupd"], CREDIT_UPD)
            v.sem_inc(S["s_var"], CREDIT_UPD)
            v.sem_inc(S["s_store"], 16)
            v.wait_ge(S["s_zero"], 5)
            v.wait_ge(S["s_ident"], 96)

            def carry_in(n, u):
                v.wait_ge(S["s_carry"], n + 1)
                v.wait_ge(S["s_rupd"], 4 * n + CREDIT_UPD)
                v.wait_ge(S["s_cattn"], 64 * n + 64)
                v.tensor_scalar(nsink[:, :], sink[:, :], -1.0, None, ALU.mult).then_inc(S["s_nsink"], 1)
                v.tensor_copy(kHH[:, 0:CHUNK], kcar[:, bass.ds(u, 1), 0].rearrange("p o c -> p (o c)").bitcast(F32))
                v.tensor_copy(kLL[:, 0:CHUNK], kcar[:, bass.ds(u, 1), 1].rearrange("p o c -> p (o c)").bitcast(F32))
                v.tensor_copy(veH[64:128, 0], vcar[64:128, bass.ds(u, 1), 0].rearrange("p o c -> p (o c)").bitcast(F32))
                v.tensor_copy(veL[64:128, 0], vcar[64:128, bass.ds(u, 1), 1].rearrange("p o c -> p (o c)").bitcast(F32)
                              ).then_inc(S["s_carin"], 1)
                v.tensor_copy(rcur[:, :], rst[:, bass.ds(u, 1)].rearrange("p o c -> p (o c)")).then_inc(S["s_rcur"], 1)

            def qkv(n, u, t):
                v.wait_ge(S["s_sq"], nth(n, 4, t))
                link(v.tensor_reduce(ss[:, :], th[:, 0:320].rearrange("p (h d) -> p h d", d=HD), AX.X, ALU.add))
                v.tensor_scalar(ms[:, :], ss[:, :], 1.0 / HD, EPS, ALU.mult, ALU.add).then_inc(S["s_ms"], 1)
                v.wait_ge(S["s_voh"], nth(n, 4, t))
                link(sub(voL[:, t], raw[:, t % 2, 320:384], voH[:, t]))
                for vo, vx, part in ((voH, veH, 0), (voL, veL, 1)):
                    v.tensor_copy(vx[0:64, t], vo[0:64, t].bitcast(F32))
                    if t < NT - 1:
                        v.tensor_copy(vx[64:128, t + 1], vo[64:128, t].bitcast(F32))
                    else:
                        v.tensor_copy(vcar[64:128, bass.ds(u, 1), part].rearrange("p o c -> p (o c)"),
                                      vo[64:128, t].bitcast(F32))
                if t >= 2:
                    v.wait_ge(S["s_tq"], nth(n, 4, t - 2))
                v.wait_ge(S["s_rstd"], nth(n, 4, t))
                v.tensor_tensor(qn[:, t % 2, 0:320].rearrange("p (h d) -> p h d", d=HD),
                                raw[:, t % 2, 0:320].rearrange("p (h d) -> p h d", d=HD),
                                rstd[:, :].unsqueeze(2).broadcast_to([P, 5, HD]), ALU.mult)
                v.tensor_tensor(qn[:, t % 2, 320:384], raw[:, t % 2, 256:320],
                                rstd[:, 4:5].broadcast_to([P, HD]), ALU.mult).then_inc(S["s_qn"], 1)

            def tql(n, t):
                v.wait_ge(S["s_tqh"], nth(n, 4, t))
                for a in range(2):
                    rows, other = slice(a * 64, a * 64 + 64), slice(64 - a * 64, 128 - a * 64)
                    v.scalar_tensor_tensor(out=qS[other, t, :, a * 64:a * 64 + 64],
                                           in0=tr[rows, 0:256].rearrange("p (c q) -> p c q", q=64),
                                           scalar=qkg[rows, 0:1], in1=qS[rows, t, :, a * 64:a * 64 + 64].bitcast(F32),
                                           op0=ALU.mult, op1=ALU.subtract)
                cols = slice(CHUNK + t * P, CHUNK + (t + 1) * P)
                v.scalar_tensor_tensor(out=kLL[:, cols], in0=tr[:, 256:384], scalar=qkg[:, 1:2],
                                       in1=kHH[:, cols].bitcast(F32), op0=ALU.mult, op1=ALU.subtract
                                       ).then_inc(S["s_tql"], 1)

            def part1(n, t):
                v.wait_ge(S["s_s"], nth(n, 4, t))
                if t == 0:
                    v.wait_ge(S["s_nsink"], nth(n, 1, 0))
                if t >= 2:
                    v.wait_ge(S["s_pt"], nth(n, 4, t - 2))
                xs = sx[:, (t % 2) * 512:(t % 2 + 1) * 512]
                bt = bias[:, 0:512] if t == 0 else bias[:, 256:768]
                v.scalar_tensor_tensor(out=xs, in0=sbk[:, :], scalar=HD ** -0.5, in1=bt, op0=ALU.mult, op1=ALU.add
                                       ).then_inc(S["s_x"], 1)
                v.wait_ge(S["s_x"], nth(n, 4, t))
                link(v.tensor_reduce(m4[:, :], xs.rearrange("p (r k) -> p r k", k=P), AX.X, ALU.max))
                b2 = lambda a: a[:, :].unsqueeze(1).broadcast_to([P, 2, 2])
                q4 = lambda a: a[:, :].rearrange("p (c h) -> p c h", c=2)
                link(v.scalar_tensor_tensor(out=q4(nm4), in0=q4(m4), scalar=-1.0, in1=b2(nsink), op0=ALU.mult,
                                            op1=ALU.min))
                v.tensor_tensor(q4(d4), q4(nm4), b2(sink), ALU.add).then_inc(S["s_nm"], 1)

            def part2(n, t):
                v.wait_ge(S["s_exp"], nth(n, 4, t))
                link(v.tensor_tensor(den[:, :], den[:, :], es[:, :], ALU.add))
                link(v.reciprocal(rc[:, :], den[:, :]))
                xs = sx[:, (t % 2) * 512:(t % 2 + 1) * 512].rearrange("p (r k) -> p r k", k=P)
                v.scalar_tensor_tensor(out=xs, in0=xs, scalar=0.5, in1=rc[:, :].unsqueeze(2).broadcast_to([P, 4, P]),
                                       op0=ALU.mult, op1=ALU.mult).then_inc(S["s_pn"], 1)

            def agg(n, i):
                v.wait_ge(S["s_agt"], nth(n, 2, i))
                v.scalar_tensor_tensor(out=gate[:, i * 512:(i + 1) * 512], in0=th[:, :], scalar=1.0, in1=jb[i % 2][:, :],
                                       op0=ALU.add, op1=ALU.mult).then_inc(S["s_gate"], 1)

            def ptl(n, t):
                v.wait_ge(S["s_pth"], nth(n, 4, t))
                sub(pTL[:, :], ptb[:, :], pTH[:, :]).then_inc(S["s_ptl"], 1)

            def mix(n, t):
                v.wait_ge(S["s_pv"], nth(n, 4, t))
                if t == 0:
                    v.wait_ge(S["s_gate"], nth(n, 2, 1))
                else:
                    v.wait_ge(S["s_mixl"], nth(n, 4, t - 1))
                for a in range(2):
                    rows = slice(a * 64, a * 64 + 64)
                    i = v.tensor_tensor(mixr[rows, :, :],
                                        ob[0:64, :].rearrange("p (h a q) -> p h a q", h=2, a=2)[:, :, a],
                                        gate[rows, :].rearrange("p (h s) -> p h s", h=2)[:, :, t * P:(t + 1) * P],
                                        ALU.mult)
                i.then_inc(S["s_mixr"], 1)

            def mixl(n, t):
                v.wait_ge(S["s_mixh"], nth(n, 4, t))
                sub(mxL[:, 0:2, t * P:(t + 1) * P], mixr[:, :, :], mxH[:, 0:2, t * P:(t + 1) * P]
                    ).then_inc(S["s_mixl"], 1)

            def rq_decay(n):
                v.wait_ge(S["s_job"], nth(n, JOBS, J_RQ) + CREDIT_JOB)
                v.wait_ge(S["s_cret"], 32 * n + 32)
                v.tensor_tensor(th[:, :].rearrange("p (t i) -> p t i", i=P),
                                jb[0][:, :].rearrange("p (t i) -> p t i", i=P),
                                cwq.unsqueeze(1).broadcast_to([P, NT, P]), ALU.mult).then_inc(S["s_qpr"], 1)

            def rql(n):
                v.wait_ge(S["s_rqh"], nth(n, 1, 0))
                for a in range(2):
                    rows = slice(a * 64, a * 64 + 64)
                    i = sub(rqL[rows, a], th[rows, :], rqH[rows, a])
                i.then_inc(S["s_rql"], 1)

            def rkl(n):
                v.wait_ge(S["s_rkh"], nth(n, 1, 0))
                sub(rkL[:, :], jb[1][:, :], rkH[:, :]).then_inc(S["s_rkl"], 1)

            def rvg(n, t):
                v.wait_ge(S["s_rvt"], nth(n, 4, t))
                bank, g = jb[t % 2], gg[:, t % 2]
                sub(rvL[:, t % 2], bank[:, 0:256], rvH[:, t % 2])
                if t >= 2:
                    v.wait_ge(S["s_mr"], nth(n, 4, t - 2))
                v.scalar_tensor_tensor(out=g, in0=th[:, 0:256], scalar=1.0, in1=bank[:, 256:512], op0=ALU.add,
                                       op1=ALU.mult).then_inc(S["s_rvg"], 1)

            def kw_am(n, t):
                v.wait_ge(S["s_kt"], nth(n, 4, t))
                if t >= 1:
                    v.wait_ge(S["s_kwl"], nth(n, 4, t - 1))
                    v.wait_ge(S["s_al"], nth(n, 4, t - 1))
                v.tensor_tensor(kwr[:, :], tr[:, 0:128], cwk, ALU.mult).then_inc(S["s_kw"], 1)
                v.wait_ge(S["s_a"], nth(n, 4, t))
                v.tensor_tensor(amr[:, :], ab[:, 0:256], cD, ALU.mult).then_inc(S["s_am"], 1)

            def kwl_al(n, t):
                v.wait_ge(S["s_kwh"], nth(n, 4, t))
                sub(kwL[:, :], kwr[:, :], kwH[:, :]).then_inc(S["s_kwl"], 1)
                v.wait_ge(S["s_ah"], nth(n, 4, t))
                sub(aL[:, :], amr[:, :], aH[:, :]).then_inc(S["s_al"], 1)

            def rl(n, t):
                v.wait_ge(S["s_rh"], nth(n, 4, t))
                sub(rL[:, :], rcur[:, :], rH[:, :]).then_inc(S["s_rl"], 1)

            def rupd(n, t, u=None):
                v.wait_ge(S["s_i"], nth(n, 4, t))
                for a in range(2):
                    rows = slice(a * 64, a * 64 + 64)
                    new = rcur[rows, :] if t < NT - 1 else rst[rows, bass.ds(u, 1)].rearrange("p o c -> p (o c)")
                    i = v.scalar_tensor_tensor(out=new, in0=rcur[rows, :], scalar=cg[rows, :],
                                               in1=ro[rows, 256 + a * P:256 + (a + 1) * P], op0=ALU.mult, op1=ALU.add)
                i.then_inc(S["s_rupd"], 1)

            def gna(n, t):
                v.wait_ge(S["s_oc"], nth(n, 4, t))
                for h in range(2):
                    i = v.bn_stats(st[:, h], oraw[:, h])
                link(i)
                v.scalar_tensor_tensor(out=gg[:, t % 2], in0=gg[:, t % 2], scalar=0.5, in1=gain[:, :], op0=ALU.mult,
                                       op1=ALU.mult)
                for h in range(2):
                    i = v.bn_aggr(mv[:, h], st[:, h])
                link(i)
                v.tensor_scalar(ve[:, :], mv[:, :, 1], EPS, None, ALU.add).then_inc(S["s_var"], 1)

            def gnb(n, t):
                v.wait_ge(S["s_grs"], nth(n, 4, t))
                for h in range(2):
                    i = v.tensor_scalar(oraw[:, h], oraw[:, h], mv[:, h, 0:1], grs[:, h:h + 1], ALU.subtract, ALU.mult)
                link(i)
                if t >= 1:
                    v.wait_ge(S["s_mt"], nth(n, 4, t - 1))
                v.tensor_tensor(mr[:, :, :], oraw[:, :, :], gg[:, t % 2].rearrange("p (h e) -> p h e", h=2), ALU.mult
                                ).then_inc(S["s_mr"], 1)

            def mtl(n, t):
                v.wait_ge(S["s_mth"], nth(n, 4, t))
                sub(mxL[:, 2:4, t * P:(t + 1) * P], tr[:, 0:256].rearrange("p (h q) -> p h q", h=2),
                    mxH[:, 2:4, t * P:(t + 1) * P]).then_inc(S["s_mtl"], 1)

            def add(n, b, i):
                v.wait_ge(S["s_job"], nth(n, JOBS, J_OUT + i) + CREDIT_JOB)
                if i == 0:
                    v.wait_ge(S["s_accin"], 16 * b + 16)
                v.wait_ge(S["s_acc"], n * 8 + (i + 1))
                a = acc[:, i // 2, (i % 2) * 512:(i % 2 + 1) * 512]
                v.tensor_tensor(a, a, jb[i % 2][:, :], ALU.add).then_inc(S["s_acc"], 1)

            def xn(b, t):
                v.wait_ge(S["s_xsq"], nth(b, 4, t))
                v.tensor_tensor(xms[:, 0:1], xss[:, 0:1], xss[:, 1:2], ALU.add).then_inc(S["s_dvex"], 1)
                v.wait_ge(S["s_dvex"], nth(b, 4, t))
                v.tensor_scalar(xms[:, 1:2], xms[:, 0:1], 1.0 / DM, EPS, ALU.mult, ALU.add).then_inc(S["s_xms"], 1)
                v.wait_ge(S["s_xr"], nth(b, 4, t))
                v.tensor_scalar(xbuf[t % 2][:, :], xbuf[t % 2][:, :], xr[:, 0:1], None, ALU.mult
                                ).then_inc(S["s_xn"], 1)

            def xl(b, t):
                for h in range(2):
                    v.wait_ge(S["s_xH"], nth(b, 8, 2 * t + h))
                    for k in range(4):
                        kk, cols = 4 * h + k, slice(t * P, (t + 1) * P)
                        i = v.scalar_tensor_tensor(out=hTL[:, kk, cols], in0=xbanks[t % 2][h][:, k * P:(k + 1) * P],
                                                   scalar=ngain[:, kk:kk + 1], in1=hTH[:, kk, cols].bitcast(F32),
                                                   op0=ALU.mult, op1=ALU.subtract)
                i.then_inc(S["s_xL"], 1)

            def unit(b, u, x_next):
                n = b * NU + u
                link_at[:] = [0, n * UNIT_LINKS]
                x = lambda f, t: f(b + 1, t) if x_next else None
                carry_in(n, u)
                qkv(n, u, 0)
                qkv(n, u, 1)
                tql(n, 0); qkv(n, u, 2)
                tql(n, 1); qkv(n, u, 3)
                tql(n, 2); part1(n, 0); agg(n, 0); part2(n, 0)
                tql(n, 3); part1(n, 1); agg(n, 1); part2(n, 1)
                ptl(n, 0); rq_decay(n); part1(n, 2); rql(n); part2(n, 2)
                ptl(n, 1); part1(n, 3); rkl(n); mix(n, 0); mixl(n, 0); part2(n, 3); rl(n, 0)
                ptl(n, 2); rvg(n, 0); mix(n, 1); kw_am(n, 0); mixl(n, 1); kwl_al(n, 0)
                ptl(n, 3); rvg(n, 1); mix(n, 2); rupd(n, 0); kw_am(n, 1); gna(n, 0); mixl(n, 2); rl(n, 1)
                kwl_al(n, 1); gnb(n, 0)
                rvg(n, 2); mix(n, 3); rupd(n, 1); kw_am(n, 2); gna(n, 1); mixl(n, 3); rl(n, 2); kwl_al(n, 2)
                mtl(n, 0); gnb(n, 1)
                rvg(n, 3); rupd(n, 2); kw_am(n, 3); gna(n, 2); rl(n, 3); kwl_al(n, 3)
                v.tensor_copy(kcar[:, bass.ds(u, 1), 0].rearrange("p o c -> p (o c)"), kHH[:, BLK:BLK + CHUNK].bitcast(F32))
                v.tensor_copy(kcar[:, bass.ds(u, 1), 1].rearrange("p o c -> p (o c)"), kLL[:, BLK:BLK + CHUNK].bitcast(F32)
                              ).then_inc(S["s_carry"], 1)
                add(n, b, 0); mtl(n, 1); gnb(n, 2); rupd(n, 3, u); gna(n, 3); x(xn, 0)
                add(n, b, 1); x(xn, 1)
                add(n, b, 2); mtl(n, 2); gnb(n, 3); x(xl, 0)
                add(n, b, 3); x(xl, 1); x(xn, 2)
                add(n, b, 4); mtl(n, 3)
                add(n, b, 5); x(xn, 3); x(xl, 2)
                add(n, b, 6)
                add(n, b, 7); x(xl, 3)
                assert link_at[0] == UNIT_LINKS, link_at

            for t in range(NT):
                xn(0, t)
                if t >= 1:
                    xl(0, t - 1)
            xl(0, NT - 1)
            with v.Fori(0, NB - 1) as b:
                with v.Fori(0, NU - 1) as u:
                    unit(b, u, False)
                unit(b, NU - 1, True)
            with v.Fori(0, NU - 1) as u:
                unit(NB - 1, u, False)
            unit(NB - 1, NU - 1, False)

        @block.tensor
        def _(pe):
            pe.sem_inc(S["s_job"], CREDIT_JOB)
            pe.wait_ge(S["s_ident"], 96)

            def mm3(o, pairs):
                last = len(pairs) - 1
                for i, ((lh, ll), (rh_, rl_)) in enumerate(pairs):
                    pe.matmul(o, lh, rh_, start=i == 0, stop=False)
                    pe.matmul(o, lh, rl_, start=False, stop=False)
                    m = pe.matmul(o, ll, rh_, start=False, stop=i == last)
                return m

            def bank_free(n, j):
                if j < 2:
                    pe.wait_ge(S["s_acc"], n * 8 + (6 + j + 1))
                elif j < 6:
                    pe.wait_ge(S["s_raw"], nth(n, 4, j - 2))
                elif j < 8:
                    pe.wait_ge(S["s_gate"], nth(n, 2, j - 6))
                elif j == 8:
                    pe.wait_ge(S["s_qpr"], nth(n, 1, 0))
                elif j == 9:
                    pe.wait_ge(S["s_rkl"], nth(n, 1, 0))
                elif j < 14:
                    pe.wait_ge(S["s_rvg"], nth(n, 4, j - 10))
                else:
                    pe.wait_ge(S["s_acc"], nth(n, 8, j - 14) + CREDIT_ACC)

            def job(n, b, j):
                bank_free(n, j)
                if j < J_AG:
                    pe.wait_ge(S["s_xL"], nth(b, 4, j))
                if j < J_OUT:
                    p = 0 if j < J_AG else 1 if j < J_RVG else 2
                    W, L = wH[p % 2], wL[p % 2]
                    pairs = []
                    for k in range(KT):
                        if j < J_AG or j >= J_RVG:
                            t = j if j < J_AG else j - J_RVG
                            cols = slice(t * P, (t + 1) * P)
                            w = W_WIDTH[p]
                            o = jb[j % 2][:, 0:w]
                            pairs.append(((hTH[:, k, cols], hTL[:, k, cols]), (W[:, k, 0:w], L[:, k, 0:w])))
                        else:
                            f = slice((j - J_AG) * P, (j - J_AG + 1) * P)
                            o = jb[j % 2][:, :]
                            pairs.append(((W[:, k, f], L[:, k, f]), (hTH[:, k, :], hTL[:, k, :])))
                    first = j in (J_QKV, J_AG, J_RVG)
                else:
                    t, h = (j - J_OUT) // 2, (j - J_OUT) % 2
                    p, W, L = 3, wH[1], wL[1]
                    if h == 0:
                        pe.wait_ge(S["s_mixl"], nth(n, 4, t))
                        pe.wait_ge(S["s_mtl"], nth(n, 4, t))
                    cols = slice(t * P, (t + 1) * P)
                    o = jb[j % 2][:, :]
                    pairs = [((mxH[:, k, cols], mxL[:, k, cols]), (W[:, 4 * h + k, :], L[:, 4 * h + k, :]))
                             for k in range(4)]
                    first = t == 0
                last = len(pairs) - 1
                for i, ((lh, ll), (rh_, rl_)) in enumerate(pairs):
                    if first:
                        s = i if p < 3 else 4 * h + i
                        pe.wait_ge(S["s_wl"], nth(n, 32, 8 * p + s) + CREDIT_WL)
                    pe.matmul(o, lh, rh_, start=i == 0, stop=False)
                    pe.matmul(o, lh, rl_, start=False, stop=False)
                    m = pe.matmul(o, ll, rh_, start=False, stop=i == last)
                m.then_inc(S["s_job"], 1)

            def TQ(n, t):
                pe.wait_ge(S["s_qn"], nth(n, 4, t))
                if t >= 1:
                    pe.wait_ge(S["s_tql"], nth(n, 4, t - 1))
                for c in range(3):
                    m = pe.transpose(tr[:, c * P:(c + 1) * P], qn[:, t % 2, c * P:(c + 1) * P], ident[:, :])
                m.then_inc(S["s_tq"], 1)

            def S_(n, t):
                pe.wait_ge(S["s_tql"], nth(n, 4, t))
                if t == 0:
                    pe.wait_ge(S["s_carin"], nth(n, 1, 0))
                else:
                    pe.wait_ge(S["s_x"], nth(n, 4, t - 1))
                for pos in range(2):
                    par = pos if t == 0 else 1 - pos
                    own = CHUNK + t * P
                    for hp in range(2):
                        q = qS[:, t, 2 * hp + par]
                        at = pos * 256 + hp * P
                        if par == 1:
                            runs = [(at, P, own)]
                        else:
                            runs = [(at, CHUNK, own), (at + CHUNK, CHUNK, own - CHUNK)]
                        for to, w, col in runs:
                            pe.matmul(sbk[:, to:to + w], q, kHH[:, col:col + w], start=True, stop=False)
                            m = pe.matmul(sbk[:, to:to + w], q, kLL[:, col:col + w], start=False, stop=True)
                m.then_inc(S["s_s"], 1)

            def PT(n, t):
                pe.wait_ge(S["s_pn"], nth(n, 4, t))
                if t >= 1:
                    pe.wait_ge(S["s_ptl"], nth(n, 4, t - 1))
                for i in range(4):
                    at = (t % 2) * 512 + i * P
                    m = pe.transpose(ptb[:, i * P:(i + 1) * P], sx[:, at:at + P], ident[:, :])
                m.then_inc(S["s_pt"], 1)

            def PV(n, t):
                pe.wait_ge(S["s_ptl"], nth(n, 4, t))
                if t >= 1:
                    pe.wait_ge(S["s_mixr"], nth(n, 4, t - 1))
                for pos in range(2):
                    par = pos if t == 0 else 1 - pos
                    vh, vl = (voH[:, t], voL[:, t]) if par else (veH[:, t], veL[:, t])
                    o = ob[0:64, :].rearrange("p (r c q) -> p r c q", c=2, q=64)[:, :, par]
                    cols = slice(pos * 256, pos * 256 + 256)
                    ph = pTH[:, cols].rearrange("p (r q) -> p r q", q=64)
                    pl = pTL[:, cols].rearrange("p (r q) -> p r q", q=64)
                    m = mm3(o, [((vh, vl), (ph, pl))])
                m.then_inc(S["s_pv"], 1)

            def KT_(n, t):
                if t == 0:
                    pe.wait_ge(S["s_rkh"], nth(n, 1, 0))
                    pe.wait_ge(S["s_tql"], nth(n, 4, 3))
                elif t < 3:
                    pe.wait_ge(S["s_kw"], nth(n, 4, t - 1))
                else:
                    pe.wait_ge(S["s_mtl"], nth(n, 4, 0))
                pe.transpose(tr[:, 0:P], kr[:, t * P:(t + 1) * P], ident[:, :]).then_inc(S["s_kt"], 1)

            def A(n, t):
                if t == 0:
                    pe.wait_ge(S["s_rql"], nth(n, 1, 0))
                    pe.wait_ge(S["s_rkl"], nth(n, 1, 0))
                else:
                    pe.wait_ge(S["s_am"], nth(n, 4, t - 1))
                cols = slice(t * P, (t + 1) * P)
                m = mm3(ab[:, 0:256].rearrange("p (a i) -> p a i", a=2),
                        [((rkH[:, cols], rkL[:, cols]), (rqH[:, :, cols], rqL[:, :, cols]))])
                m.then_inc(S["s_a"], 1)

            def I(n, t):
                pe.wait_ge(S["s_rl"], nth(n, 4, t))
                pe.wait_ge(S["s_kwl"], nth(n, 4, t))
                pe.wait_ge(S["s_al"], nth(n, 4, t))
                pe.wait_ge(S["s_rvg"], nth(n, 4, t))
                if t >= 1:
                    pe.wait_ge(S["s_oc"], nth(n, 4, t - 1))
                cols = slice(t * P, (t + 1) * P)
                for a in range(2):
                    e = slice(a * P, (a + 1) * P)
                    mm3(ro[:, e], [((rqH[:, a, cols], rqL[:, a, cols]), (rH[:, :], rL[:, :])),
                                   ((aH[:, e], aL[:, e]), (rvH[:, t % 2, e], rvL[:, t % 2, e]))])
                m = mm3(ro[:, 256:512], [((kwH[:, :], kwL[:, :]), (rvH[:, t % 2], rvL[:, t % 2]))])
                m.then_inc(S["s_i"], 1)

            def MT(n, t):
                pe.wait_ge(S["s_mr"], nth(n, 4, t))
                if t < 2:
                    pe.wait_ge(S["s_kw"], nth(n, 4, t + 2))
                else:
                    pe.wait_ge(S["s_mtl"], nth(n, 4, t - 1))
                for h in range(2):
                    m = pe.transpose(tr[:, h * P:(h + 1) * P], mr[:, h], ident[:, :])
                m.then_inc(S["s_mt"], 1)

            steps = {"TQ": TQ, "S": S_, "PT": PT, "PV": PV, "KT": KT_, "A": A, "I": I, "MT": MT}

            def XT(b, t):
                pe.wait_ge(S["s_xn"], nth(b, 4, t))
                if t >= 2:
                    pe.wait_ge(S["s_xL"], nth(b, 4, t - 2))
                for k in range(KT):
                    m = pe.transpose(xbanks[t % 2][k // 4][:, (k % 4) * P:(k % 4 + 1) * P],
                                     xbuf[t % 2][:, k * P:(k + 1) * P], ident[:, :])
                m.then_inc(S["s_xT"], 1)

            def unit(b, u, x_next):
                n = b * NU + u
                for j in range(JOBS + 1):
                    for what, t in STEPS.get(j, ()):
                        steps[what](n, t)
                    if x_next and j in X_STEPS:
                        XT(b + 1, X_STEPS[j])
                    if j < JOBS:
                        job(n, b, j)

            for t in range(NT):
                XT(0, t)
            with pe.Fori(0, NB - 1) as b:
                with pe.Fori(0, NU - 1) as u:
                    unit(b, u, False)
                unit(b, NU - 1, True)
            with pe.Fori(0, NU - 1) as u:
                unit(NB - 1, u, False)
            unit(NB - 1, NU - 1, False)


_OUT_SHAPE = (1, SEQ, DM)


def kernel(**inputs):
    import numpy as np
    import concourse.bacc as bacc
    from concourse.bass_utils import run_bass_kernel_spmd as run

    f32 = np.float32
    slopes = (2.0 ** (-8.0 * (np.arange(HEADS) + 1.0) / HEADS)).astype(f32)
    q = np.arange(CHUNK)[:, None]
    ki = np.arange(2 * CHUNK)[None, :]
    dist = np.abs(q + CHUNK - ki).astype(f32)
    even = np.concatenate([dist[:, CHUNK:], dist[:, :CHUNK]], axis=1)
    c_bias = np.zeros((KVH, P, 512), f32)
    c_bias0 = np.zeros((NB, KVH, P, 256), f32)
    for g in range(KVH):
        for hp in range(2):
            for a in range(2):
                s = -slopes[4 * g + 2 * hp + a]
                rows = slice(64 * a, 64 * a + 64)
                c_bias[g, rows, hp * P:(hp + 1) * P] = s * dist
                c_bias[g, rows, 256 + hp * P:256 + (hp + 1) * P] = s * even
                c_bias0[:, g, rows, hp * P:(hp + 1) * P] = s * even
                c_bias0[0, g, rows, hp * P + CHUNK:(hp + 1) * P] = -1e30
    c_ret = np.zeros((NU, P, 513), f32)
    i = np.arange(P)
    scale = HD ** -0.5
    for h in range(RET_HEADS):
        u, a = h // 2, h % 2
        g = 1.0 - 2.0 ** (-5.0 - h)
        di = g ** np.abs(i[None, :] - i[:, None]) * (i[:, None] // CHUNK <= i[None, :] // CHUNK)
        c_ret[u, :, a * P:(a + 1) * P] = scale * di * g ** (-(i[None, :] + 1.0))
        rows = slice(64 * a, 64 * a + 64)
        c_ret[u, rows, 256:384] = g ** (i[None, :] + 1.0)
        c_ret[u, :, 384 + 64 * a:384 + 64 * a + 64] = (scale * g ** (127.0 - i))[:, None]
        c_ret[u, rows, 512] = g ** 128.0

    nc = bacc.Bacc("TRN2", target_bir_lowering=False, num_devices=1, dynamic_dma_scratch_size=1024)
    names = ("x", "norm_gain", "w_in", "q_norm_gain", "k_norm_gain", "sink_logits", "ret_norm_gain", "w_out")
    arrays = {f"{n}_dram": np.ascontiguousarray(inputs[n]) for n in names}
    arrays.update(c_bias0_dram=c_bias0, c_bias_dram=c_bias, c_ret_dram=c_ret, c_ident_dram=np.eye(P, dtype=f32))
    args = [nc.dram_tensor(n, a.shape, F32, kind="ExternalInput").ap() for n, a in arrays.items()]
    out = nc.dram_tensor("out_dram", _OUT_SHAPE, F32, kind="ExternalOutput").ap()
    build(nc, *args, out)
    r = run(nc, [arrays], core_ids=[0])
    return r.results[0]["out_dram"]
```

```python
from contextlib import ExitStack

import concourse.bass as bass
from concourse import mybir

F32 = mybir.dt.float32
F32R = mybir.dt.float32r
ALU = mybir.AluOpType
ACT = mybir.ActivationFunctionType
AX = mybir.AxisListType

P = 128
SEQ, DM = 2048, 1024
CHUNK = 64
HD = 64
HEADS, KVH = 16, 4
RET_HEADS, RV = 8, 128
EPS = 1e-6
BLK = 512
NB = SEQ // BLK
NT = BLK // P
KT = DM // P
NU = KVH
C_AQ, C_AK, C_AV, C_AG, C_RQ, C_RK, C_RV, C_RG = 0, 1024, 1280, 1536, 2560, 3072, 3584, 4608
D_ATTN = 1024

J_QKV, J_AG, J_RQ, J_RK, J_RVG, J_OUT, JOBS = 0, 4, 6, 7, 8, 12, 20
W_SUBS = 8
W_PANELS = 4
W_WIDTH = [384, 512, 512, 512]
W_DMAS = [3, 3, 2, 1]
STEPS = {
    3: [("TQ", 0)], 4: [("TQ", 1)], 5: [("TQ", 2), ("S", 0)], 6: [("TQ", 3), ("S", 1)],
    7: [("PT", 0), ("S", 2)], 8: [("PT", 1), ("PV", 0), ("S", 3)],
    9: [("PT", 2), ("PV", 1), ("A", 0)],
    10: [("A", 1), ("I", 0), ("PV", 2)],
    11: [("PT", 3), ("I", 1), ("A", 2)],
    12: [("MT", 0), ("PV", 3), ("A", 3)],
    13: [("I", 2)], 14: [("MT", 1)], 15: [("I", 3)], 16: [("MT", 2)], 18: [("MT", 3)],
}
X_STEPS = {15: 0, 16: 1, 19: 2, 20: 3}
STAGES = 4
CREDIT_JOB, CREDIT_ACC, CREDIT_SAVE, CREDIT_UPD, CREDIT_WL, CREDIT_STORE = JOBS, 2 * NT, 1, NT, 32, 64


def nth(n, per_unit, j):
    return n * per_unit + (j + 1)


def build(nc, x, norm_gain, w_in, q_gain, k_gain, sinks, ret_gain, w_out, c_bias0, c_bias, c_ret, c_ident, out):
    w_in_v = w_in.rearrange("(k p) n -> p k n", p=P)
    w_out_v = w_out.rearrange("(k p) n -> p k n", p=P)
    sinks_v = sinks.rearrange("(h a) -> a h", a=2)

    with ExitStack() as ctx:
        def sb(name, shape, dt=F32):
            return ctx.enter_context(nc.sbuf_tensor(name, shape, dt))

        def pb(name):
            return ctx.enter_context(nc.psum_tensor(name, [P, 512], F32))

        def sem(name):
            return ctx.enter_context(nc.semaphore(name))

        hTH, hTL = sb("hTH", [P, KT, BLK], F32R), sb("hTL", [P, KT, BLK], F32R)
        wH = [sb(f"wH{i}", [P, W_SUBS, 512], F32R) for i in range(2)]
        wL = [sb(f"wL{i}", [P, W_SUBS, 512], F32R) for i in range(2)]
        stage = sb("stage", [P, STAGES, 2, 512])
        acc = sb("acc", [P, NT, DM])
        mxH, mxL = sb("mxH", [P, 4, BLK], F32R), sb("mxL", [P, 4, BLK], F32R)
        gate = sb("gate", [P, 2 * BLK])
        sx = sb("sx", [P, 2 * BLK])
        th = sb("th", [P, BLK])
        rawqn = sb("rawqn", [P, 4, 384])
        raw = rawqn[:, 0:2]
        qn = rawqn[:, 2:4]
        rawqn_flat = rawqn[:, :, :].rearrange("p a b -> p (a b)")
        xbuf = [rawqn_flat[:, 0:DM], sx[:, :]]
        obt = rawqn_flat[0:64, DM:DM + 512]
        qS = sb("qS", [P, NT, 4, P], F32R)
        kHL = sb("kHL", [P, 2, CHUNK + BLK], F32R)
        vodd = sb("vodd", [P, NT, 2, HD], F32R)
        veven = sb("veven", [P, NT, 2, HD], F32R)
        kcar = sb("kcar", [P, NU, 2, CHUNK], F32R)
        vcar = sb("vcar", [P, NU, 2, HD], F32R)
        pTH, pTL = sb("pTH", [P, 512], F32R), sb("pTL", [P, 512], F32R)
        mixr = sb("mixr", [P, 2, P])
        bias = sb("bias", [P, 512])
        sink, nsink = sb("sink", [P, 2]), sb("nsink", [P, 2])
        m4, nm4, d4, den, es, rc = (sb(n_, [P, 4]) for n_ in ("m4", "nm4", "d4", "den", "es", "rc"))
        ss, ms, rstd = sb("ss", [P, 5]), sb("ms", [P, 5]), sb("rstd", [P, 5])
        mhalf = sb("mhalf", [P, 8])
        rqH, rqL = sb("rqH", [P, 2, BLK], F32R), sb("rqL", [P, 2, BLK], F32R)
        rkH, rkL = sb("rkH", [P, BLK], F32R), sb("rkL", [P, BLK], F32R)
        kr = sb("kr", [P, BLK])
        rv = sb("rv", [P, 2, 2, 2, RV], F32R)
        gg = sb("gg", [P, 3, 2 * RV])
        kwr, kwH, kwL = sb("kwr", [P, P]), sb("kwH", [P, P], F32R), sb("kwL", [P, P], F32R)
        amr, aH, aL = sb("amr", [P, 2 * P]), sb("aH", [P, 2 * P], F32R), sb("aL", [P, 2 * P], F32R)
        rst = sb("rst", [P, NU, RV])
        rcur, rHL = sb("rcur", [P, RV]), sb("rHL", [P, 2, RV], F32R)
        oraw, mr = sb("oraw", [P, 2, RV]), sb("mr", [P, 2, RV])
        st, mv, ve, grs = sb("st", [P, 2, 6]), sb("mv", [P, 2, 2]), sb("ve", [P, 2]), sb("grs", [P, 2])
        cret = sb("cret", [P, 513])
        cD, cwq, cwk, cg = cret[:, 0:256], cret[:, 256:384], cret[:, 384:512], cret[:, 512:513]
        gain = sb("gain", [P, 2 * RV])
        ident = sb("ident", [P, P])
        ngain = sb("ngain", [P, KT])
        qkg = sb("qkg", [P, 2])
        xss, xms, xr = sb("xss", [P, 1]), sb("xms", [P, 1]), sb("xr", [P, 1])

        jb = [pb("jb0"), pb("jb1")]
        tr, ptb, ob, ab = pb("tr"), pb("ptb"), pb("ob"), pb("ab")
        s2 = ctx.enter_context(nc.psum_tensor("s2", [P, 1024], F32))
        sbk, ro = s2[:, 0:512], s2[:, 512:1024]
        s_parts = s2[:, :].rearrange("p (c r h k) -> p c r h k", c=2, r=2, h=2)

        names = """s_ident s_gains s_qkg s_mhalf s_zero s_x0 s_x1 s_first0 s_first1 s_first2 s_first3 s_xsq s_xms s_xr s_xn s_xT s_xH s_xL s_accin s_store
            s_w0 s_w1 s_w2 s_w3 s_wh s_wl s_job s_cattn s_cret s_raw s_sq s_voh s_ms s_rstd s_qn s_tq s_tqh s_tql
            s_s s_x s_nm s_exp s_pn s_pt s_pth s_ptl s_pv s_obc s_mixr s_mixh s_mixl s_agt s_gate
            s_qpr s_rqh s_rql s_rkh s_rkl s_rvt s_rvg s_kw s_kwh s_kwl s_a s_am s_ah s_al
            s_i s_rupd s_oh s_oc s_ggm s_rh s_rl s_rcur s_var s_grs s_mr s_mt s_mth s_mtl s_acc s_nsink s_carin s_carry
            s_dve""".split()
        S = {name: sem(name) for name in names}
        s_x = [S["s_x0"], S["s_x1"]]
        s_first = [S["s_first0"], S["s_first1"], S["s_first2"], S["s_first3"]]
        s_w = [S["s_w0"], S["s_w1"], S["s_w2"], S["s_w3"]]
        ro_parts = ro[:, :].rearrange("p (a h e) -> p a h e", a=2, h=2)
        xbanks = ((ptb, ob), (sbk, ab))
        block = ctx.enter_context(nc.Block())

        @block.sync
        def _(sp):
            def panel(n, u, p, chunks=range(4)):
                for c in chunks:
                    sp.wait_ge(S["s_wl"], nth(n, 32, 8 * (p - 1) + 2 * c + 1) + CREDIT_WL)
                    dst, done = stage[:, c], s_w[c]
                    if p < 3:
                        strips = (((0, 256, C_AQ), (256, 64, C_AK), (320, 64, C_AV)),
                                  ((0, 256, C_AG), (256, 128, C_RQ), (384, 128, C_RK)),
                                  ((0, 256, C_RV), (256, 256, C_RG)))[p]
                        for at, w, col in strips:
                            sp.dma_start(dst[:, :, at:at + w],
                                         w_in_v[:, 2 * c:2 * c + 2, bass.ds(u * w + col, w)]).then_inc(done, 16)
                    else:
                        base = (c % 2) * KT
                        sp.dma_start(dst[:, :, :], w_out_v[:, bass.ds(u * 2 + base, 2),
                                                           (c // 2) * 512:(c // 2 + 1) * 512]).then_inc(done, 16)

            def x_tile(b, t):
                if t >= 2:
                    sp.wait_ge(S["s_xT"], nth(b, 4, t - 2))
                else:
                    sp.wait_ge(S[("s_tq", "s_pt")[t]], b * NU * NT)
                sp.dma_start(xbuf[t % 2], x[0, bass.ds(b * BLK + t * P, P), :]).then_inc(s_x[t % 2], 16)

            def rest(b, u, first=False, x_next=False):
                n = b * NU + u
                sp.wait_ge(S["s_carry"], n + 1)
                sp.dma_start(bias[:, 0:256], c_bias0[b, u]).then_inc(S["s_cattn"], 16)
                sp.dma_start(bias[:, 256:512], c_bias[u]).then_inc(S["s_cattn"], 16)
                for a in range(2):
                    sp.dma_start(sink[a * 64:a * 64 + 64, :],
                                 sinks_v[a, bass.ds(u * 2, 2)].partition_broadcast(64),
                                 allow_slow_non_contiguous=True).then_inc(S["s_cattn"], 16)
                sp.wait_ge(S["s_var"], 4 * n + CREDIT_UPD)
                sp.wait_ge(S["s_ggm"], 4 * n + CREDIT_UPD)
                sp.dma_start(cret[:, :], c_ret[u]).then_inc(S["s_cret"], 16)
                sp.dma_start(gain[:, :], ret_gain[bass.ds(u * 256, 256)].partition_broadcast(P)).then_inc(S["s_cret"], 16)
                panel(n, u, 1)
                if first:
                    sp.wait_ge(S["s_store"], 64 * b + 64)
                    sp.wait_ge(S["s_xn"], NT)
                    sp.dma_start(acc[:, :, :], x[0, bass.ds(b * BLK, BLK), :].rearrange("(t p) d -> p t d", p=P)
                                 ).then_inc(S["s_accin"], 16)
                panel(n, u, 2)
                if x_next:
                    x_tile(b + 1, 0)
                panel(n, u, 3)

            def store(b):
                for t in range(NT):
                    sp.wait_ge(S["s_acc"], b * 32 + (24 + 2 * (t + 1) + CREDIT_ACC))
                    sp.dma_start(out[0, bass.ds(b * BLK + t * P, P), :], acc[:, t]).then_inc(S["s_store"], 16)

            def units(b, x_next):
                rest(b, 0, first=True)
                panel(b * NU + 1, 1, 0)
                with sp.Fori(1, NU - 1) as u:
                    rest(b, u)
                    panel(b * NU + u + 1, u + 1, 0)
                rest(b, NU - 1, x_next=x_next)

            for t in range(NT):
                sp.dma_start(acc[:, t], x[0, t * P:(t + 1) * P, :]).then_inc(s_first[t], 16)
                if t == 0:
                    sp.dma_start(ident[:, :], c_ident).then_inc(S["s_ident"], 16)
                panel(0, 0, 0, (t,))
                if t == 0:
                    sp.dma_start(ngain[:, :], norm_gain.rearrange("(k p) -> p k", p=P), allow_slow_non_contiguous=True
                                 ).then_inc(S["s_gains"], 16)
            for half in range(2):
                rows = slice(half * HD, half * HD + HD)
                sp.dma_start(qkg[rows, 0:1], q_gain.rearrange("(d o) -> d o", o=1)).then_inc(S["s_qkg"], 16)
                sp.dma_start(qkg[rows, 1:2], k_gain.rearrange("(d o) -> d o", o=1)).then_inc(S["s_qkg"], 16)
            with sp.Fori(0, NB - 1) as b:
                units(b, True)
                x_tile(b + 1, 1)
                panel((b + 1) * NU, 0, 0)
                x_tile(b + 1, 2)
                x_tile(b + 1, 3)
                store(b)
            units(NB - 1, False)
            store(NB - 1)
            sp.wait_ge(S["s_store"], 64 * (NB + 1))

        @block.gpsimd
        def _(pool):
            pool.memset(mhalf[:, :], -0.5).then_inc(S["s_mhalf"], 1)
            pool.sem_inc(S["s_wl"], CREDIT_WL)
            pool.sem_inc(S["s_ggm"], CREDIT_UPD)
            pool.wait_ge(S["s_mhalf"], 1)

            def wl(n, p, subs):
                for s in subs:
                    pool.wait_ge(S["s_wh"], nth(n, 32, 8 * p + s))
                    w = W_WIDTH[p]
                    pool.tensor_tensor(wL[p % 2][:, s, 0:w], stage[:, s // 2, s % 2, 0:w],
                                       wH[p % 2][:, s, 0:w].bitcast(F32), ALU.subtract).then_inc(S["s_wl"], 1)

            def rpow(n, t):
                pool.wait_ge(S["s_ms"], nth(n, 4, t))
                pool.tensor_tensor(rstd[:, :], ms[:, :], mhalf[:, 0:5], ALU.pow).then_inc(S["s_rstd"], 1)

            def rql(n):
                pool.wait_ge(S["s_wl"], nth(n, 32, 21) + CREDIT_WL)
                pool.wait_ge(S["s_rqh"], nth(n, 1, 0))
                for a in range(2):
                    rows = slice(a * 64, a * 64 + 64)
                    pool.tensor_tensor(rqL[rows, a], th[rows, :], rqH[rows, a].bitcast(F32), ALU.subtract
                                       ).then_inc(S["s_rql"], 1)
                    pool.wait_ge(S["s_rql"], nth(n, 2, a))

            def rkl(n):
                pool.wait_ge(S["s_rkh"], nth(n, 1, 0))
                pool.tensor_tensor(rkL[:, :], kr[:, :], rkH[:, :].bitcast(F32), ALU.subtract).then_inc(S["s_rkl"], 1)

            def mixl(n, t):
                pool.wait_ge(S["s_mixh"], nth(n, 4, t))
                cols = slice(t * P, (t + 1) * P)
                pool.tensor_tensor(mxL[:, 0:2, cols], mixr[:, :, :], mxH[:, 0:2, cols].bitcast(F32), ALU.subtract
                                   ).then_inc(S["s_mixl"], 1)

            def ggm(n, t):
                pool.wait_ge(S["s_rvg"], nth(n, 4, t))
                if t == 0:
                    pool.wait_ge(S["s_cret"], 32 * n + 32)
                pool.tensor_tensor(gg[:, t % 3], gg[:, t % 3], gain[:, :], ALU.mult).then_inc(S["s_ggm"], 1)

            def gpow(n, t):
                pool.wait_ge(S["s_var"], nth(n, 4, t) + CREDIT_UPD)
                pool.tensor_tensor(grs[:, :], ve[:, :], mhalf[:, 0:2], ALU.pow).then_inc(S["s_grs"], 1)

            def xpow(b, t):
                pool.wait_ge(S["s_xms"], nth(b, 4, t))
                pool.tensor_tensor(xr[:, :], xms[:, :], mhalf[:, 0:1], ALU.pow).then_inc(S["s_xr"], 1)

            def unit(b, u, nxt, x_next):
                n = b * NU + u
                rpow(n, 0); wl(n, 1, (0, 1, 2))
                rpow(n, 1); wl(n, 1, (3, 4, 5))
                rpow(n, 2); wl(n, 1, (6, 7))
                rpow(n, 3); wl(n, 2, range(6)); rql(n)
                wl(n, 2, (6, 7)); rkl(n); mixl(n, 0); wl(n, 3, (0, 1)); mixl(n, 1); ggm(n, 0)
                wl(n, 3, (2, 3)); ggm(n, 1); wl(n, 3, (4, 5)); gpow(n, 0); mixl(n, 2); ggm(n, 2)
                wl(n, 3, (6, 7)); ggm(n, 3)
                x = lambda t: xpow(b + 1, t) if x_next else None
                w = lambda *subs: wl(n + 1, 0, subs) if nxt else None
                gpow(n, 1); mixl(n, 3); x(0)
                gpow(n, 2); x(1); w(0, 1)
                gpow(n, 3); w(2, 3); w(4, 5); x(2); w(6, 7); x(3)

            for t in range(NT):
                xpow(0, t)
                wl(0, 0, (2 * t, 2 * t + 1))
            with pool.Fori(0, NB - 1) as b:
                with pool.Fori(0, NU - 1) as u:
                    unit(b, u, True, False)
                unit(b, NU - 1, True, True)
            with pool.Fori(0, NU - 1) as u:
                unit(NB - 1, u, True, False)
            unit(NB - 1, NU - 1, False, False)

        @block.scalar
        def _(act):
            def wh(n, p, subs):
                for s in subs:
                    c = s // 2
                    if s == subs[0]:
                        last = {0: J_OUT - 1 - JOBS, 1: JOBS - 1 - JOBS, 2: J_AG - 1, 3: J_RK}[p]
                        act.wait_ge(S["s_job"], nth(n, JOBS, last) + CREDIT_JOB)
                    if s % 2 == 0 or s == subs[0]:
                        done = sum(W_DMAS[:p + 1])
                        act.wait_ge(s_w[c], n * (16 * sum(W_DMAS)) + 16 * done)
                    w = W_WIDTH[p]
                    act.activation(wH[p % 2][:, s, 0:w], stage[:, c, s % 2, 0:w], ACT.Copy).then_inc(S["s_wh"], 1)

            def qkv(n, t):
                act.wait_ge(S["s_job"], nth(n, JOBS, J_QKV + t) + CREDIT_JOB)
                if t >= 2:
                    act.wait_ge(S["s_qn"], nth(n, 4, t - 2))
                act.activation(raw[:, t % 2], jb[t % 2][:, 0:384], ACT.Copy).then_inc(S["s_raw"], 1)
                act.wait_ge(S["s_raw"], nth(n, 4, t))
                if t >= 1:
                    act.wait_ge(S["s_ms"], nth(n, 4, t - 1))
                act.activation(th[:, 0:320], raw[:, t % 2, 0:320], ACT.Square).then_inc(S["s_sq"], 1)
                act.activation(vodd[:, t, 0], raw[:, t % 2, 320:384], ACT.Copy).then_inc(S["s_voh"], 1)

            def tqh(n, t):
                act.wait_ge(S["s_tq"], nth(n, 4, t))
                for a in range(2):
                    rows = slice(a * 64, a * 64 + 64)
                    act.activation(qS[rows, t, :, a * 64:a * 64 + 64],
                                   tr[rows, 0:256].rearrange("p (c q) -> p c q", q=64), ACT.Copy, scale=qkg[rows, 0:1])
                act.activation(kHL[:, 0, CHUNK + t * P:CHUNK + (t + 1) * P], tr[:, 256:384], ACT.Copy,
                               scale=qkg[:, 1:2]).then_inc(S["s_tqh"], 1)

            def ag(n, i):
                act.wait_ge(S["s_job"], nth(n, JOBS, J_AG + i) + CREDIT_JOB)
                if i == 0:
                    act.wait_ge(S["s_ms"], nth(n, 4, 3))
                else:
                    act.wait_ge(S["s_gate"], nth(n, 2, 0))
                act.activation(th[:, :], jb[i % 2][:, :], ACT.Tanh, scale=0.5).then_inc(S["s_agt"], 1)

            def exps(n, t):
                act.wait_ge(S["s_nm"], nth(n, 4, t))
                for i in range(4):
                    v = sx[:, (t % 2) * 512 + i * P:(t % 2) * 512 + (i + 1) * P]
                    act.activation(v, v, ACT.Exp, bias=nm4[:, i:i + 1], accum_out=den[:, i:i + 1])
                act.activation(es[:, :], d4[:, :], ACT.Exp).then_inc(S["s_exp"], 1)

            def pth(n, t):
                act.wait_ge(S["s_pt"], nth(n, 4, t))
                if t >= 1:
                    act.wait_ge(S["s_pv"], nth(n, 4, t - 1))
                act.activation(pTH[:, :], ptb[:, :], ACT.Copy).then_inc(S["s_pth"], 1)

            def rqh(n):
                act.wait_ge(S["s_qpr"], nth(n, 1, 0))
                for a in range(2):
                    rows = slice(a * 64, a * 64 + 64)
                    i = act.activation(rqH[rows, a], th[rows, :], ACT.Copy)
                i.then_inc(S["s_rqh"], 1)

            def rk(n):
                act.wait_ge(S["s_job"], nth(n, JOBS, J_RK) + CREDIT_JOB)
                act.activation(kr[:, :], jb[1][:, :], ACT.Copy)
                act.activation(rkH[:, :], jb[1][:, :], ACT.Copy).then_inc(S["s_rkh"], 1)

            def rvg(n, t):
                act.wait_ge(S["s_job"], nth(n, JOBS, J_RVG + t) + CREDIT_JOB)
                if t >= 2:
                    act.wait_ge(S["s_i"], nth(n, 4, t - 2))
                act.activation(rv[:, t % 2, :, 0], jb[t % 2][:, 0:256].rearrange("p (a e) -> p a e", a=2), ACT.Copy)
                if t == 0:
                    act.wait_ge(S["s_rql"], nth(n, 2, 1))
                else:
                    act.wait_ge(S["s_rvg"], nth(n, 4, t - 1))
                act.activation(th[:, 0:256], jb[t % 2][:, 256:512], ACT.Tanh, scale=0.5).then_inc(S["s_rvt"], 1)

            def obcopy(n, t):
                act.wait_ge(S["s_pv"], nth(n, 4, t))
                if t >= 1:
                    act.wait_ge(S["s_mixr"], nth(n, 4, t - 1))
                act.activation(obt[:, :], ob[64:128, :], ACT.Copy).then_inc(S["s_obc"], 1)

            def mixh(n, t):
                act.wait_ge(S["s_mixr"], nth(n, 4, t))
                act.activation(mxH[:, 0:2, t * P:(t + 1) * P], mixr[:, :, :], ACT.Copy).then_inc(S["s_mixh"], 1)

            def kwh_ah(n, t):
                act.wait_ge(S["s_kw"], nth(n, 4, t))
                if t >= 1:
                    act.wait_ge(S["s_i"], nth(n, 4, t - 1))
                act.activation(kwH[:, :], kwr[:, :], ACT.Copy).then_inc(S["s_kwh"], 1)
                act.wait_ge(S["s_am"], nth(n, 4, t))
                act.activation(aH[:, :], amr[:, :], ACT.Copy).then_inc(S["s_ah"], 1)

            def rh(n, t):
                if t == 0:
                    act.wait_ge(S["s_rcur"], nth(n, 1, 0))
                else:
                    act.wait_ge(S["s_rupd"], nth(n, 4, t - 1) + CREDIT_UPD)
                act.activation(rHL[:, 0], rcur[:, :], ACT.Copy).then_inc(S["s_rh"], 1)

            def ocopy(n, t):
                act.wait_ge(S["s_i"], nth(n, 4, t))
                if t >= 1:
                    act.wait_ge(S["s_mr"], nth(n, 4, t - 1))
                act.activation(oraw[:, :, :], ro_parts[:, :, 0], ACT.Copy).then_inc(S["s_oh"], 1)

            def mth(n, t):
                act.wait_ge(S["s_mt"], nth(n, 4, t))
                act.activation(mxH[:, 2:4, t * P:(t + 1) * P], tr[:, 0:256].rearrange("p (h q) -> p h q", h=2),
                               ACT.Copy).then_inc(S["s_mth"], 1)

            def xsq(b, t, first=False):
                if first:
                    act.wait_ge(s_first[t], 16)
                else:
                    act.wait_ge(s_x[t % 2], b * 32 + (16 * (t // 2 + 1) - 32))
                if t >= 1:
                    act.wait_ge(S["s_xms"], nth(b, 4, t - 1))
                elif not first:
                    act.wait_ge(S["s_mixr"], b * NU * NT)
                act.activation(gate[:, :], acc[:, t] if first else xbuf[t % 2], ACT.Square, accum_out=xss[:, :]).then_inc(S["s_xsq"], 1)

            def xh(b, t):
                act.wait_ge(S["s_xT"], nth(b, 4, t))
                for h in range(2):
                    for k in range(4):
                        i = act.activation(hTH[:, 4 * h + k, t * P:(t + 1) * P], xbanks[t % 2][h][:, k * P:(k + 1) * P],
                                           ACT.Copy, scale=ngain[:, 4 * h + k:4 * h + k + 1])
                    i.then_inc(S["s_xH"], 1)

            def unit(b, u, nxt, x_next):
                n = b * NU + u
                x = lambda f, t: f(b + 1, t) if x_next else None
                w = lambda *subs: wh(n + 1, 0, list(subs)) if nxt else None
                qkv(n, 0); wh(n, 1, [0, 1, 2])
                qkv(n, 1); wh(n, 1, [3, 4, 5])
                tqh(n, 0); qkv(n, 2); wh(n, 1, [6, 7])
                tqh(n, 1); qkv(n, 3); wh(n, 2, [0, 1])
                tqh(n, 2); rh(n, 0); ag(n, 0); wh(n, 2, [2, 3]); exps(n, 0)
                tqh(n, 3); ag(n, 1); wh(n, 2, [4, 5]); exps(n, 1)
                pth(n, 0); rqh(n); wh(n, 2, [6, 7]); exps(n, 2)
                pth(n, 1); rk(n); obcopy(n, 0); mixh(n, 0); wh(n, 3, [0, 1]); exps(n, 3)
                pth(n, 2); rvg(n, 0); kwh_ah(n, 0); obcopy(n, 1); mixh(n, 1); wh(n, 3, [2, 3])
                rvg(n, 1); rh(n, 1); kwh_ah(n, 1); obcopy(n, 2); ocopy(n, 0); mixh(n, 2); wh(n, 3, [4, 5])
                pth(n, 3); rvg(n, 2); rh(n, 2); kwh_ah(n, 2); ocopy(n, 1); wh(n, 3, [6, 7])
                rvg(n, 3); mth(n, 0); obcopy(n, 3); mixh(n, 3)
                x(xsq, 0); rh(n, 3); kwh_ah(n, 3); ocopy(n, 2); x(xsq, 1)
                mth(n, 1); w(0, 1)
                ocopy(n, 3); w(2, 3); x(xh, 0); mth(n, 2)
                x(xh, 1); w(4, 5); x(xsq, 2); w(6, 7); mth(n, 3)
                x(xsq, 3); x(xh, 2)
                x(xh, 3)

            for t in range(NT):
                xsq(0, t, first=True)
                wh(0, 0, [2 * t, 2 * t + 1])
                if t == 1:
                    act.wait_ge(S["s_gains"], 16)
                    xh(0, 0)
                    xh(0, 1)
                if t == 3:
                    xh(0, 2)
            xh(0, NT - 1)
            act.wait_ge(S["s_qkg"], 64)
            with act.Fori(0, NB - 1) as b:
                with act.Fori(0, NU - 1) as u:
                    unit(b, u, True, False)
                unit(b, NU - 1, True, True)
            with act.Fori(0, NU - 1) as u:
                unit(NB - 1, u, True, False)
            unit(NB - 1, NU - 1, False, False)

        @block.vector
        def _(v):
            UNIT_LINKS = 44
            link_at = [0, 0]

            def link(ins):
                ins.then_inc(S["s_dve"], 1)
                link_at[0] += 1
                v.wait_ge(S["s_dve"], link_at[1] + link_at[0])

            def sub(out, a, h):
                return v.tensor_tensor(out, a, h.bitcast(F32), ALU.subtract)

            v.memset(rst[:, :, :], 0.0).then_inc(S["s_zero"], 1)
            v.memset(rqH[:, :, :].bitcast(F32), 0.0).then_inc(S["s_zero"], 1)
            v.memset(rqL[:, :, :].bitcast(F32), 0.0).then_inc(S["s_zero"], 1)
            v.memset(kcar[:, :, :, :].bitcast(F32), 0.0).then_inc(S["s_zero"], 1)
            v.memset(vcar[:, :, :, :].bitcast(F32), 0.0).then_inc(S["s_zero"], 1)
            v.sem_inc(S["s_acc"], CREDIT_ACC)
            v.sem_inc(S["s_carry"], CREDIT_SAVE)
            v.sem_inc(S["s_rupd"], CREDIT_UPD)
            v.sem_inc(S["s_var"], CREDIT_UPD)
            v.sem_inc(S["s_store"], CREDIT_STORE)
            v.wait_ge(S["s_zero"], 5)

            def carry_in(n, u):
                v.wait_ge(S["s_carry"], n + 1)
                v.wait_ge(S["s_rupd"], 4 * n + CREDIT_UPD)
                v.wait_ge(S["s_cattn"], 64 * n + 64)
                v.tensor_scalar(nsink[:, :], sink[:, :], -1.0, None, ALU.mult).then_inc(S["s_nsink"], 1)
                v.tensor_copy(kHL[:, :, 0:CHUNK], kcar[:, bass.ds(u, 1)].rearrange("p o h c -> p (o h) c").bitcast(F32))
                v.tensor_copy(veven[0:64, 0], vcar[0:64, bass.ds(u, 1)].rearrange("p o h c -> p (o h) c").bitcast(F32)
                              ).then_inc(S["s_carin"], 1)
                v.tensor_copy(rcur[:, :], rst[:, bass.ds(u, 1)].rearrange("p o c -> p (o c)")).then_inc(S["s_rcur"], 1)

            def qkv(n, u, t):
                v.wait_ge(S["s_sq"], nth(n, 4, t))
                link(v.tensor_reduce(ss[:, :], th[:, 0:320].rearrange("p (h d) -> p h d", d=HD), AX.X, ALU.add))
                v.tensor_scalar(ms[:, :], ss[:, :], 1.0 / HD, EPS, ALU.mult, ALU.add).then_inc(S["s_ms"], 1)
                v.wait_ge(S["s_voh"], nth(n, 4, t))
                link(sub(vodd[:, t, 1], raw[:, t % 2, 320:384], vodd[:, t, 0]))
                v.tensor_copy(veven[64:128, t], vodd[0:64, t].bitcast(F32))
                if t < NT - 1:
                    v.tensor_copy(veven[0:64, t + 1], vodd[64:128, t].bitcast(F32))
                else:
                    v.tensor_copy(vcar[0:64, bass.ds(u, 1)].rearrange("p o h c -> p (o h) c"), vodd[64:128, t].bitcast(F32))
                if t >= 2:
                    v.wait_ge(S["s_tq"], nth(n, 4, t - 2))
                v.wait_ge(S["s_rstd"], nth(n, 4, t))
                v.tensor_tensor(qn[:, t % 2, 0:320].rearrange("p (h d) -> p h d", d=HD),
                                raw[:, t % 2, 0:320].rearrange("p (h d) -> p h d", d=HD),
                                rstd[:, :].unsqueeze(2).broadcast_to([P, 5, HD]), ALU.mult)
                v.tensor_tensor(qn[:, t % 2, 320:384], raw[:, t % 2, 256:320],
                                rstd[:, 4:5].broadcast_to([P, HD]), ALU.mult).then_inc(S["s_qn"], 1)

            def tql(n, t):
                v.wait_ge(S["s_tqh"], nth(n, 4, t))
                for a in range(2):
                    rows, other = slice(a * 64, a * 64 + 64), slice(64 - a * 64, 128 - a * 64)
                    v.scalar_tensor_tensor(out=qS[other, t, :, a * 64:a * 64 + 64],
                                           in0=tr[rows, 0:256].rearrange("p (c q) -> p c q", q=64),
                                           scalar=qkg[rows, 0:1], in1=qS[rows, t, :, a * 64:a * 64 + 64].bitcast(F32),
                                           op0=ALU.mult, op1=ALU.subtract)
                cols = slice(CHUNK + t * P, CHUNK + (t + 1) * P)
                v.scalar_tensor_tensor(out=kHL[:, 1, cols], in0=tr[:, 256:384], scalar=qkg[:, 1:2],
                                       in1=kHL[:, 0, cols].bitcast(F32), op0=ALU.mult, op1=ALU.subtract
                                       ).then_inc(S["s_tql"], 1)

            def part1(n, t):
                v.wait_ge(S["s_s"], nth(n, 4, t))
                if t == 0:
                    v.wait_ge(S["s_nsink"], nth(n, 1, 0))
                if t >= 2:
                    v.wait_ge(S["s_pt"], nth(n, 4, t - 2))
                xs = sx[:, (t % 2) * 512:(t % 2 + 1) * 512]
                four = lambda a: a.rearrange("p (c r k) -> p c r k", c=2, r=2)
                bt = four(bias[:, :]) if t == 0 else bias[:, 256:512].rearrange("p (r k) -> p r k", r=2
                                                                                ).unsqueeze(1).broadcast_to([P, 2, 2, P])
                link(v.scalar_tensor_tensor(out=four(xs), in0=s_parts[:, :, :, 0], scalar=HD ** -0.5, in1=bt,
                                            op0=ALU.mult, op1=ALU.add))
                v.scalar_tensor_tensor(out=four(xs), in0=s_parts[:, :, :, 1], scalar=HD ** -0.5, in1=four(xs),
                                       op0=ALU.mult, op1=ALU.add).then_inc(S["s_x"], 1)
                v.wait_ge(S["s_x"], nth(n, 4, t))
                link(v.tensor_reduce(m4[:, :], xs.rearrange("p (r k) -> p r k", k=P), AX.X, ALU.max))
                b2 = lambda a: a[:, :].unsqueeze(1).broadcast_to([P, 2, 2])
                q4 = lambda a: a[:, :].rearrange("p (c h) -> p c h", c=2)
                link(v.scalar_tensor_tensor(out=q4(nm4), in0=q4(m4), scalar=-1.0, in1=b2(nsink), op0=ALU.mult,
                                            op1=ALU.min))
                v.tensor_tensor(q4(d4), q4(nm4), b2(sink), ALU.add).then_inc(S["s_nm"], 1)

            def part2(n, t):
                v.wait_ge(S["s_exp"], nth(n, 4, t))
                link(v.tensor_tensor(den[:, :], den[:, :], es[:, :], ALU.add))
                link(v.reciprocal(rc[:, :], den[:, :]))
                xs = sx[:, (t % 2) * 512:(t % 2 + 1) * 512].rearrange("p (r k) -> p r k", k=P)
                v.scalar_tensor_tensor(out=xs, in0=xs, scalar=0.5, in1=rc[:, :].unsqueeze(2).broadcast_to([P, 4, P]),
                                       op0=ALU.mult, op1=ALU.mult).then_inc(S["s_pn"], 1)

            def agg(n, i):
                v.wait_ge(S["s_agt"], nth(n, 2, i))
                v.scalar_tensor_tensor(out=gate[:, i * 512:(i + 1) * 512], in0=th[:, :], scalar=1.0, in1=jb[i % 2][:, :],
                                       op0=ALU.add, op1=ALU.mult).then_inc(S["s_gate"], 1)

            def ptl(n, t):
                v.wait_ge(S["s_pth"], nth(n, 4, t))
                sub(pTL[:, :], ptb[:, :], pTH[:, :]).then_inc(S["s_ptl"], 1)

            def mix(n, t):
                v.wait_ge(S["s_obc"], nth(n, 4, t))
                link(v.tensor_tensor(obt[:, :], obt[:, :], ob[0:64, :], ALU.add))
                if t == 0:
                    v.wait_ge(S["s_gate"], nth(n, 2, 1))
                else:
                    v.wait_ge(S["s_mixl"], nth(n, 4, t - 1))
                for a in range(2):
                    rows = slice(a * 64, a * 64 + 64)
                    i = v.tensor_tensor(mixr[rows, :, :],
                                        obt[:, :].rearrange("p (h a q) -> p h a q", h=2, a=2)[:, :, a],
                                        gate[rows, :].rearrange("p (h s) -> p h s", h=2)[:, :, t * P:(t + 1) * P],
                                        ALU.mult)
                i.then_inc(S["s_mixr"], 1)

            def rq_decay(n):
                v.wait_ge(S["s_job"], nth(n, JOBS, J_RQ) + CREDIT_JOB)
                v.wait_ge(S["s_cret"], 32 * n + 32)
                v.tensor_tensor(th[:, :].rearrange("p (t i) -> p t i", i=P),
                                jb[0][:, :].rearrange("p (t i) -> p t i", i=P),
                                cwq.unsqueeze(1).broadcast_to([P, NT, P]), ALU.mult).then_inc(S["s_qpr"], 1)

            def rvg(n, t):
                v.wait_ge(S["s_rvt"], nth(n, 4, t))
                bank, g = jb[t % 2], gg[:, t % 3]
                sub(rv[:, t % 2, :, 1], bank[:, 0:256].rearrange("p (a e) -> p a e", a=2), rv[:, t % 2, :, 0])
                if t >= 3:
                    v.wait_ge(S["s_mr"], nth(n, 4, t - 3))
                v.scalar_tensor_tensor(out=g, in0=th[:, 0:256], scalar=1.0, in1=bank[:, 256:512], op0=ALU.add,
                                       op1=ALU.mult).then_inc(S["s_rvg"], 1)

            def kw_am(n, t):
                v.wait_ge(S["s_a"], nth(n, 4, t))
                if t >= 1:
                    v.wait_ge(S["s_kwl"], nth(n, 4, t - 1))
                    v.wait_ge(S["s_al"], nth(n, 4, t - 1))
                v.tensor_tensor(kwr[:, :], ab[:, 256:384], cwk, ALU.mult).then_inc(S["s_kw"], 1)
                v.tensor_tensor(amr[:, :], ab[:, 0:256], cD, ALU.mult).then_inc(S["s_am"], 1)

            def kwl_al(n, t):
                v.wait_ge(S["s_kwh"], nth(n, 4, t))
                sub(kwL[:, :], kwr[:, :], kwH[:, :]).then_inc(S["s_kwl"], 1)
                v.wait_ge(S["s_ah"], nth(n, 4, t))
                sub(aL[:, :], amr[:, :], aH[:, :]).then_inc(S["s_al"], 1)

            def rl(n, t):
                v.wait_ge(S["s_rh"], nth(n, 4, t))
                sub(rHL[:, 1], rcur[:, :], rHL[:, 0]).then_inc(S["s_rl"], 1)

            def rupd(n, t, u=None):
                v.wait_ge(S["s_i"], nth(n, 4, t))
                for a in range(2):
                    rows = slice(a * 64, a * 64 + 64)
                    new = rcur[rows, :] if t < NT - 1 else rst[rows, bass.ds(u, 1)].rearrange("p o c -> p (o c)")
                    i = v.scalar_tensor_tensor(out=new, in0=rcur[rows, :], scalar=cg[rows, :],
                                               in1=sbk[rows, a * P:(a + 1) * P], op0=ALU.mult, op1=ALU.add)
                i.then_inc(S["s_rupd"], 1)

            def gna(n, t):
                v.wait_ge(S["s_oh"], nth(n, 4, t))
                v.tensor_tensor(oraw[:, :, :], oraw[:, :, :], ro_parts[:, :, 1], ALU.add).then_inc(S["s_oc"], 1)
                v.wait_ge(S["s_oc"], nth(n, 4, t))
                for h in range(2):
                    i = v.bn_stats(st[:, h], oraw[:, h])
                link(i)

            def gnv(n, t):
                for h in range(2):
                    i = v.bn_aggr(mv[:, h], st[:, h])
                link(i)
                v.tensor_scalar(ve[:, :], mv[:, :, 1], 4.0, 4.0 * EPS, ALU.mult, ALU.add).then_inc(S["s_var"], 1)

            def gnb(n, t):
                v.wait_ge(S["s_grs"], nth(n, 4, t))
                v.wait_ge(S["s_ggm"], nth(n, 4, t) + CREDIT_UPD)
                for h in range(2):
                    i = v.tensor_scalar(oraw[:, h], oraw[:, h], mv[:, h, 0:1], grs[:, h:h + 1], ALU.subtract, ALU.mult)
                link(i)
                if t >= 1:
                    v.wait_ge(S["s_mt"], nth(n, 4, t - 1))
                v.tensor_tensor(mr[:, :, :], oraw[:, :, :], gg[:, t % 3].rearrange("p (h e) -> p h e", h=2), ALU.mult
                                ).then_inc(S["s_mr"], 1)

            def mtl(n, t):
                v.wait_ge(S["s_mth"], nth(n, 4, t))
                sub(mxL[:, 2:4, t * P:(t + 1) * P], tr[:, 0:256].rearrange("p (h q) -> p h q", h=2),
                    mxH[:, 2:4, t * P:(t + 1) * P]).then_inc(S["s_mtl"], 1)

            def add(n, b, i):
                v.wait_ge(S["s_job"], nth(n, JOBS, J_OUT + i) + CREDIT_JOB)
                if i == 0:
                    v.wait_ge(S["s_accin"], 16 * b + 16)
                v.wait_ge(S["s_acc"], n * 8 + (i + 1))
                a = acc[:, i // 2, (i % 2) * 512:(i % 2 + 1) * 512]
                v.tensor_tensor(a, a, jb[i % 2][:, :], ALU.add).then_inc(S["s_acc"], 1)

            def xms_(b, t):
                v.wait_ge(S["s_xsq"], nth(b, 4, t))
                v.tensor_scalar(xms[:, :], xss[:, :], 1.0 / DM, EPS, ALU.mult, ALU.add).then_inc(S["s_xms"], 1)

            def xn(b, t, first=False):
                if first and t >= 2:
                    v.wait_ge(S["s_xT"], t - 1)
                v.wait_ge(S["s_xr"], nth(b, 4, t))
                v.tensor_scalar(xbuf[t % 2], acc[:, t] if first else xbuf[t % 2], xr[:, 0:1], None, ALU.mult).then_inc(S["s_xn"], 1)

            def xl(b, t):
                for h in range(2):
                    v.wait_ge(S["s_xH"], nth(b, 8, 2 * t + h))
                    for k in range(4):
                        kk, cols = 4 * h + k, slice(t * P, (t + 1) * P)
                        i = v.scalar_tensor_tensor(out=hTL[:, kk, cols], in0=xbanks[t % 2][h][:, k * P:(k + 1) * P],
                                                   scalar=ngain[:, kk:kk + 1], in1=hTH[:, kk, cols].bitcast(F32),
                                                   op0=ALU.mult, op1=ALU.subtract)
                i.then_inc(S["s_xL"], 1)

            def unit(b, u, x_next):
                n = b * NU + u
                link_at[:] = [0, n * UNIT_LINKS]
                x = lambda f, t: f(b + 1, t) if x_next else None
                carry_in(n, u)
                qkv(n, u, 0)
                qkv(n, u, 1)
                tql(n, 0); qkv(n, u, 2)
                tql(n, 1); qkv(n, u, 3)
                tql(n, 2); rl(n, 0); part1(n, 0); agg(n, 0); part2(n, 0)
                tql(n, 3); part1(n, 1); agg(n, 1); part2(n, 1)
                rq_decay(n); ptl(n, 0); part1(n, 2); part2(n, 2)
                ptl(n, 1); mix(n, 0); part1(n, 3)
                ptl(n, 2); kw_am(n, 0); kwl_al(n, 0); rvg(n, 0); mix(n, 1); part2(n, 3)
                rupd(n, 0); kw_am(n, 1); rl(n, 1); rvg(n, 1); kwl_al(n, 1); mix(n, 2); gna(n, 0)
                ptl(n, 3); gnv(n, 0); rupd(n, 1); kw_am(n, 2); rvg(n, 2); rl(n, 2); kwl_al(n, 2); gnb(n, 0); gna(n, 1)
                rvg(n, 3); gnv(n, 1); mtl(n, 0); kw_am(n, 3); mix(n, 3); gnb(n, 1)
                v.tensor_copy(kcar[:, bass.ds(u, 1)].rearrange("p o h c -> p (o h) c"),
                              kHL[:, :, BLK:BLK + CHUNK].bitcast(F32)).then_inc(S["s_carry"], 1)
                rupd(n, 2); add(n, b, 0); rl(n, 3); kwl_al(n, 3); x(xms_, 0); gna(n, 2)
                mtl(n, 1); gnv(n, 2); add(n, b, 1); x(xn, 0); x(xms_, 1)
                add(n, b, 2); gnb(n, 2); rupd(n, 3, u); gna(n, 3)
                x(xn, 1); mtl(n, 2); gnv(n, 3); add(n, b, 3); x(xl, 0)
                add(n, b, 4); gnb(n, 3); x(xms_, 2); x(xl, 1)
                mtl(n, 3); add(n, b, 5); x(xn, 2); x(xms_, 3)
                add(n, b, 6); x(xn, 3); x(xl, 2)
                add(n, b, 7); x(xl, 3)
                assert link_at[0] == UNIT_LINKS, link_at

            for t in range(NT):
                xms_(0, t)
                xn(0, t, first=True)
                if t == 1:
                    v.wait_ge(S["s_gains"], 16)
                    xl(0, 0)
                    xl(0, 1)
                if t == 3:
                    xl(0, 2)
            xl(0, NT - 1)
            v.wait_ge(S["s_qkg"], 64)
            with v.Fori(0, NB - 1) as b:
                with v.Fori(0, NU - 1) as u:
                    unit(b, u, False)
                unit(b, NU - 1, True)
            with v.Fori(0, NU - 1) as u:
                unit(NB - 1, u, False)
            unit(NB - 1, NU - 1, False)

        @block.tensor
        def _(pe):
            pe.sem_inc(S["s_job"], CREDIT_JOB)
            pe.wait_ge(S["s_ident"], 16)

            def mm3(o, pairs):
                last = len(pairs) - 1
                for i, ((lh, ll), (rh_, rl_)) in enumerate(pairs):
                    pe.matmul(o, lh, rh_, start=i == 0, stop=False)
                    pe.matmul(o, lh, rl_, start=False, stop=False)
                    m = pe.matmul(o, ll, rh_, start=False, stop=i == last)
                return m

            def bank_free(n, j):
                if j < 2:
                    pe.wait_ge(S["s_acc"], n * 8 + (6 + j + 1))
                elif j < 6:
                    pe.wait_ge(S["s_raw"], nth(n, 4, j - 2))
                elif j < 8:
                    pe.wait_ge(S["s_gate"], nth(n, 2, j - 6))
                elif j == 8:
                    pe.wait_ge(S["s_qpr"], nth(n, 1, 0))
                elif j == 9:
                    pe.wait_ge(S["s_rkh"], nth(n, 1, 0))
                elif j < 14:
                    pe.wait_ge(S["s_rvg"], nth(n, 4, j - 10))
                else:
                    pe.wait_ge(S["s_acc"], nth(n, 8, j - 14) + CREDIT_ACC)

            def job(n, b, j):
                bank_free(n, j)
                if j < J_AG:
                    pe.wait_ge(S["s_xL"], nth(b, 4, j))
                if j < J_OUT:
                    p = 0 if j < J_AG else 1 if j < J_RVG else 2
                    W, L = wH[p % 2], wL[p % 2]
                    pairs = []
                    for k in range(KT):
                        if j < J_AG or j >= J_RVG:
                            t = j if j < J_AG else j - J_RVG
                            cols = slice(t * P, (t + 1) * P)
                            w = W_WIDTH[p]
                            o = jb[j % 2][:, 0:w]
                            pairs.append(((hTH[:, k, cols], hTL[:, k, cols]), (W[:, k, 0:w], L[:, k, 0:w])))
                        else:
                            f = slice((j - J_AG) * P, (j - J_AG + 1) * P)
                            o = jb[j % 2][:, :]
                            pairs.append(((W[:, k, f], L[:, k, f]), (hTH[:, k, :], hTL[:, k, :])))
                    first = j in (J_QKV, J_AG, J_RVG)
                else:
                    t, h = (j - J_OUT) // 2, (j - J_OUT) % 2
                    p, W, L = 3, wH[1], wL[1]
                    if h == 0:
                        pe.wait_ge(S["s_mixl"], nth(n, 4, t))
                    cols = slice(t * P, (t + 1) * P)
                    o = jb[j % 2][:, :]
                    pairs = [((mxH[:, k, cols], mxL[:, k, cols]), (W[:, 4 * h + k, :], L[:, 4 * h + k, :]))
                             for k in range(4)]
                    first = t == 0
                last = len(pairs) - 1
                for i, ((lh, ll), (rh_, rl_)) in enumerate(pairs):
                    if first:
                        s = i if p < 3 else 4 * h + i
                        pe.wait_ge(S["s_wl"], nth(n, 32, 8 * p + s) + CREDIT_WL)
                    if j >= J_OUT and h == 0 and i == 2:
                        pe.wait_ge(S["s_mtl"], nth(n, 4, t))
                    pe.matmul(o, lh, rh_, start=i == 0, stop=False)
                    pe.matmul(o, lh, rl_, start=False, stop=False)
                    m = pe.matmul(o, ll, rh_, start=False, stop=i == last)
                m.then_inc(S["s_job"], 1)

            def TQ(n, t):
                pe.wait_ge(S["s_qn"], nth(n, 4, t))
                if t >= 1:
                    pe.wait_ge(S["s_tql"], nth(n, 4, t - 1))
                for c in range(3):
                    m = pe.transpose(tr[:, c * P:(c + 1) * P], qn[:, t % 2, c * P:(c + 1) * P], ident[:, :])
                m.then_inc(S["s_tq"], 1)

            def S_(n, t):
                pe.wait_ge(S["s_tql"], nth(n, 4, t))
                if t == 0:
                    pe.wait_ge(S["s_carin"], nth(n, 1, 0))
                else:
                    pe.wait_ge(S["s_x"], nth(n, 4, t - 1))
                for par in range(2):
                    win = slice((2 * t + par) * CHUNK, (2 * t + par + 2) * CHUNK)
                    for hp in range(2):
                        m = pe.matmul(s_parts[:, par, hp], qS[:, t, 2 * hp + par], kHL[:, :, win], start=True, stop=True)
                m.then_inc(S["s_s"], 1)

            def PT(n, t):
                pe.wait_ge(S["s_pn"], nth(n, 4, t))
                if t >= 1:
                    pe.wait_ge(S["s_ptl"], nth(n, 4, t - 1))
                for i in range(4):
                    at = (t % 2) * 512 + i * P
                    m = pe.transpose(ptb[:, i * P:(i + 1) * P], sx[:, at:at + P], ident[:, :])
                m.then_inc(S["s_pt"], 1)

            def PV(n, t):
                pe.wait_ge(S["s_ptl"], nth(n, 4, t))
                if t >= 1:
                    pe.wait_ge(S["s_mixr"], nth(n, 4, t - 1))
                for par in range(2):
                    v = (vodd if par else veven)[:, t].rearrange("p h d -> p (h d)")
                    o = ob[:, :].rearrange("p (r c q) -> p r c q", c=2, q=64)[:, :, par]
                    for i, pT in enumerate((pTH, pTL)):
                        m = pe.matmul(o, v, pT[:, par * 256:(par + 1) * 256].rearrange("p (r q) -> p r q", q=64),
                                      start=i == 0, stop=i == 1)
                m.then_inc(S["s_pv"], 1)

            def A(n, t):
                if t == 0:
                    pe.wait_ge(S["s_rql"], nth(n, 2, 1))
                    pe.wait_ge(S["s_rkl"], nth(n, 1, 0))
                else:
                    pe.wait_ge(S["s_am"], nth(n, 4, t - 1))
                cols = slice(t * P, (t + 1) * P)
                pe.transpose(ab[:, 256:384], kr[:, cols], ident[:, :])
                m = mm3(ab[:, 0:256].rearrange("p (a i) -> p a i", a=2),
                        [((rkH[:, cols], rkL[:, cols]), (rqH[:, :, cols], rqL[:, :, cols]))])
                m.then_inc(S["s_a"], 1)

            def I(n, t):
                pe.wait_ge(S["s_rl"], nth(n, 4, t))
                pe.wait_ge(S["s_kwl"], nth(n, 4, t))
                pe.wait_ge(S["s_al"], nth(n, 4, t))
                pe.wait_ge(S["s_rvg"], nth(n, 4, t))
                if t >= 1:
                    pe.wait_ge(S["s_oc"], nth(n, 4, t - 1))
                cols = slice(t * P, (t + 1) * P)
                for a in range(2):
                    o, e, v = ro[:, a * 256:(a + 1) * 256], slice(a * P, (a + 1) * P), rv[:, t % 2, a]
                    both = lambda w: w.rearrange("p h e -> p (h e)")
                    pe.matmul(o, rqH[:, a, cols], both(rHL[:, :, :]), start=True, stop=False)
                    pe.matmul(o, aH[:, e], both(v), start=False, stop=False)
                    pe.matmul(o[:, 0:P], rqL[:, a, cols], rHL[:, 0], start=False, stop=False)
                    pe.matmul(o[:, 0:P], aL[:, e], v[:, 0], start=False, stop=True)
                m = mm3(sbk[:, 0:256].rearrange("p (a e) -> p a e", a=2),
                        [((kwH[:, :], kwL[:, :]), (rv[:, t % 2, :, 0], rv[:, t % 2, :, 1]))])
                m.then_inc(S["s_i"], 1)

            def MT(n, t):
                pe.wait_ge(S["s_mr"], nth(n, 4, t))
                if t >= 1:
                    pe.wait_ge(S["s_mtl"], nth(n, 4, t - 1))
                for h in range(2):
                    m = pe.transpose(tr[:, h * P:(h + 1) * P], mr[:, h], ident[:, :])
                m.then_inc(S["s_mt"], 1)

            steps = {"TQ": TQ, "S": S_, "PT": PT, "PV": PV, "A": A, "I": I, "MT": MT}

            def XT(b, t):
                pe.wait_ge(S["s_xn"], nth(b, 4, t))
                if t >= 2:
                    pe.wait_ge(S["s_xL"], nth(b, 4, t - 2))
                for k in range(KT):
                    m = pe.transpose(xbanks[t % 2][k // 4][:, (k % 4) * P:(k % 4 + 1) * P],
                                     xbuf[t % 2][:, k * P:(k + 1) * P], ident[:, :])
                m.then_inc(S["s_xT"], 1)

            def unit(b, u, x_next):
                n = b * NU + u
                for j in range(JOBS + 1):
                    for what, t in STEPS.get(j, ()):
                        steps[what](n, t)
                    if x_next and j in X_STEPS:
                        XT(b + 1, X_STEPS[j])
                    if j < JOBS:
                        job(n, b, j)

            for t in range(NT):
                XT(0, t)
            with pe.Fori(0, NB - 1) as b:
                with pe.Fori(0, NU - 1) as u:
                    unit(b, u, False)
                unit(b, NU - 1, True)
            with pe.Fori(0, NU - 1) as u:
                unit(NB - 1, u, False)
            unit(NB - 1, NU - 1, False)


_OUT_SHAPE = (1, SEQ, DM)


def kernel(**inputs):
    import numpy as np
    import concourse.bacc as bacc
    from concourse.bass_utils import run_bass_kernel_spmd as run

    f32 = np.float32
    slopes = (2.0 ** (-8.0 * (np.arange(HEADS) + 1.0) / HEADS)).astype(f32)
    q = np.arange(CHUNK)[:, None]
    ki = np.arange(2 * CHUNK)[None, :]
    dist = np.abs(q + CHUNK - ki).astype(f32)
    c_bias = np.zeros((KVH, P, 256), f32)
    c_bias0 = np.zeros((NB, KVH, P, 256), f32)
    for g in range(KVH):
        for hp in range(2):
            for a in range(2):
                s = -slopes[4 * g + 2 * hp + a]
                rows = slice(64 * a, 64 * a + 64)
                c_bias[g, rows, hp * P:(hp + 1) * P] = s * dist
                c_bias0[:, g, rows, hp * P:(hp + 1) * P] = s * dist
                c_bias0[0, g, rows, hp * P:hp * P + CHUNK] = -1e30
    c_ret = np.zeros((NU, P, 513), f32)
    i = np.arange(P)
    scale = HD ** -0.5
    for h in range(RET_HEADS):
        u, a = h // 2, h % 2
        g = 1.0 - 2.0 ** (-5.0 - h)
        di = g ** np.abs(i[None, :] - i[:, None]) * (i[:, None] // CHUNK <= i[None, :] // CHUNK)
        c_ret[u, :, a * P:(a + 1) * P] = scale * di * g ** (-(i[None, :] + 1.0))
        rows = slice(64 * a, 64 * a + 64)
        c_ret[u, rows, 256:384] = g ** (i[None, :] + 1.0)
        c_ret[u, :, 384 + 64 * a:384 + 64 * a + 64] = (scale * g ** (127.0 - i))[:, None]
        c_ret[u, rows, 512] = g ** 128.0

    nc = bacc.Bacc("TRN2", target_bir_lowering=False, num_devices=1, dynamic_dma_scratch_size=1024)
    names = ("x", "norm_gain", "w_in", "q_norm_gain", "k_norm_gain", "sink_logits", "ret_norm_gain", "w_out")
    arrays = {f"{n}_dram": np.ascontiguousarray(inputs[n]) for n in names}
    arrays.update(c_bias0_dram=c_bias0, c_bias_dram=c_bias, c_ret_dram=c_ret, c_ident_dram=np.eye(P, dtype=f32))
    args = [nc.dram_tensor(n, a.shape, F32, kind="ExternalInput").ap() for n, a in arrays.items()]
    out = nc.dram_tensor("out_dram", _OUT_SHAPE, F32, kind="ExternalOutput").ap()
    build(nc, *args, out)
    r = run(nc, [arrays], core_ids=[0])
    return r.results[0]["out_dram"]
```
